# Optimizing a Trainium2 kernel written in Bass

```python
import math
import jax, jax.numpy as jnp
from jax import lax
import numpy as np

D_MODEL = 1024
BATCH = 1
SEQ = 1024
DEPTH = 2

N_A_LAYERS = DEPTH // 2
N_B_LAYERS = DEPTH - N_A_LAYERS
RET_HEADS = 4
RET_QK_DIM = D_MODEL // RET_HEADS
RET_V_DIM = 2 * D_MODEL // RET_HEADS
RET_CHUNK = 128
ROPE_BASE = 10000.0
SWA_HEADS = 16
SWA_KV_HEADS = 4
SWA_GROUP = SWA_HEADS // SWA_KV_HEADS
SWA_HEAD_DIM = 64
WINDOW = 128
BLOCK = WINDOW
REL_BUCKETS = 32
REL_MAX_DIST = 128
D_FF = 2816
CONV_WIDTH = 3
NORM_EPS = 1e-6

kernel_name = "yoco_retention_swa_sink_hybrid"

def rmsnorm(x, g):
    x32 = x.astype(jnp.float32)
    y = x32 * lax.rsqrt(jnp.mean(x32 * x32, axis=-1, keepdims=True) + NORM_EPS)
    return (y * g.astype(jnp.float32)).astype(x.dtype)

def adaln_in(x, g, shift, scale):
    return rmsnorm(x, g) * (1 + scale[:, None, :]) + shift[:, None, :]

def rotary(x, pos):
    d = x.shape[-1]
    half = d // 2
    inv = ROPE_BASE ** (-jnp.arange(half, dtype=jnp.float32) / half)
    ang = pos.astype(jnp.float32)[:, None] * inv[None, :]
    cos = jnp.cos(ang)[None, :, None, :]
    sin = jnp.sin(ang)[None, :, None, :]
    x32 = x.astype(jnp.float32)
    x1, x2 = x32[..., :half], x32[..., half:]
    return jnp.concatenate([x1 * cos - x2 * sin, x2 * cos + x1 * sin], axis=-1)

def retention(h, w_in, w_out):
    B, S, _ = h.shape
    H, dk, dv, C = RET_HEADS, RET_QK_DIM, RET_V_DIM, RET_CHUNK
    NC = S // C
    proj = h @ w_in
    q, k, v, g = jnp.split(proj, [H * dk, 2 * H * dk, 2 * H * dk + H * dv], axis=-1)
    pos = jnp.arange(S)
    q = rotary(q.reshape(B, S, H, dk), pos)
    k = rotary(k.reshape(B, S, H, dk), pos) * (dk ** -0.5)
    v = v.reshape(B, S, H, dv).astype(jnp.float32)

    def to_chunks(t):
        return t.reshape(B, NC, C, H, t.shape[-1]).transpose(1, 0, 3, 2, 4)

    log_gamma = jnp.log(1.0 - 2.0 ** (-5.0 - jnp.arange(H, dtype=jnp.float32)))
    idx = jnp.arange(C, dtype=jnp.float32)
    diff = idx[:, None] - idx[None, :]
    dmask = jnp.where(diff[None] >= 0, jnp.exp(jnp.maximum(diff, 0.0)[None] * log_gamma[:, None, None]), 0.0)
    xi = jnp.exp((idx[None, :] + 1.0) * log_gamma[:, None])
    zeta = jnp.exp((C - 1.0 - idx[None, :]) * log_gamma[:, None])
    g_chunk = jnp.exp(C * log_gamma)

    def step(R, qkv):
        qc, kc, vc = qkv
        s = jnp.einsum('bhqd,bhkd->bhqk', qc, kc) * dmask[None]
        inner = jnp.einsum('bhqk,bhkv->bhqv', s, vc)
        cross = jnp.einsum('bhqd,bhdv->bhqv', qc, R) * xi[None, :, :, None]
        R_new = R * g_chunk[None, :, None, None] + jnp.einsum('bhkd,bhkv->bhdv', kc, vc * zeta[None, :, :, None])
        return R_new, inner + cross

    R0 = jnp.zeros((B, H, dk, dv), jnp.float32)
    _, o = lax.scan(step, R0, (to_chunks(q), to_chunks(k), to_chunks(v)))
    o = o.transpose(1, 0, 3, 2, 4).reshape(B, S, H, dv)
    mu = jnp.mean(o, axis=-1, keepdims=True)
    var = jnp.mean(jnp.square(o - mu), axis=-1, keepdims=True)
    o = ((o - mu) * lax.rsqrt(var + NORM_EPS)).reshape(B, S, H * dv).astype(h.dtype)
    return (jax.nn.silu(g) * o) @ w_out

def shared_kv(x, g, shift, scale, w_kv):
    B, S, _ = x.shape
    NB = S // BLOCK
    h = adaln_in(x, g, shift, scale)
    k, v = jnp.split(h @ w_kv, 2, axis=-1)

    def band(t):
        t = t.reshape(B, S, SWA_KV_HEADS, SWA_HEAD_DIM)
        t = jnp.pad(t, ((0, 0), (BLOCK, 0), (0, 0), (0, 0)))
        tb = t.reshape(B, NB + 1, BLOCK, SWA_KV_HEADS, SWA_HEAD_DIM)
        return jnp.concatenate([tb[:, :-1], tb[:, 1:]], axis=2)

    return band(k), band(v)

def rel_bias_band(table):
    i = jnp.arange(BLOCK)[:, None]
    j = jnp.arange(2 * BLOCK)[None, :]
    dist = i + BLOCK - j
    n = jnp.maximum(dist, 0)
    max_exact = REL_BUCKETS // 2
    large = max_exact + (jnp.log(jnp.maximum(n, 1).astype(jnp.float32) / max_exact)
                         / math.log(REL_MAX_DIST / max_exact) * (REL_BUCKETS - max_exact)).astype(jnp.int32)
    large = jnp.minimum(large, REL_BUCKETS - 1)
    bucket = jnp.where(n < max_exact, n, large)
    bias = table[bucket].astype(jnp.float32)
    bias = bias.transpose(2, 0, 1).reshape(SWA_KV_HEADS, SWA_GROUP, BLOCK, 2 * BLOCK)
    win = (dist >= 0) & (dist < WINDOW)
    return bias, win

def swa_sink_attention(h, w_q, w_o, sinks, k_band, v_band, bias, mask):
    B, S, _ = h.shape
    NB = S // BLOCK
    q = (h @ w_q).reshape(B, NB, BLOCK, SWA_KV_HEADS, SWA_GROUP, SWA_HEAD_DIM)
    s = jnp.einsum('bnqhgd,bnkhd->bnhgqk', q, k_band).astype(jnp.float32) * (SWA_HEAD_DIM ** -0.5)
    s = s + bias[None, None]
    s = jnp.where(mask[None, :, None, None], s, -jnp.inf)
    sink = sinks.astype(jnp.float32).reshape(SWA_KV_HEADS, SWA_GROUP)[None, None, :, :, None, None]
    m = jnp.maximum(jnp.max(s, axis=-1, keepdims=True), sink)
    e = jnp.exp(s - m)
    p = e / (jnp.sum(e, axis=-1, keepdims=True) + jnp.exp(sink - m))
    o = jnp.einsum('bnhgqk,bnkhd->bnqhgd', p.astype(v_band.dtype), v_band)
    return o.reshape(B, S, SWA_HEADS * SWA_HEAD_DIM) @ w_o

def conv_ffn(h, w_up, conv_w, conv_b, w_down):
    S = h.shape[1]
    u = h @ w_up
    u_pad = jnp.pad(u, ((0, 0), (CONV_WIDTH - 1, 0), (0, 0)))
    uc = conv_b + sum(conv_w[j] * u_pad[:, j:j + S] for j in range(CONV_WIDTH))
    gate, val = jnp.split(uc, 2, axis=-1)
    return (jax.nn.silu(gate) * val) @ w_down

def setup_inputs(seed: int = 0) -> dict:
    key = jax.random.key(seed)
    ks = jax.random.split(key, 24)
    D, F = D_MODEL, D_FF
    nrm = lambda k, shape, s: jax.random.normal(k, shape, jnp.float32) * s
    ret_in_cols = 2 * RET_HEADS * RET_QK_DIM + 2 * RET_HEADS * RET_V_DIM
    return {
        "x": nrm(ks[0], (BATCH, SEQ, D), 1.0),
        "c": nrm(ks[1], (BATCH, D), 1.0),
        "norm_g": 1.0 + nrm(ks[2], (DEPTH, 4, D), 0.05),
        "ada_w": nrm(ks[3], (DEPTH, D, 6 * D), 0.1 * D ** -0.5),
        "ada_b": nrm(ks[4], (DEPTH, 6 * D), 0.01),
        "ret_w_in": nrm(ks[5], (N_A_LAYERS, D, ret_in_cols), D ** -0.5),
        "ret_w_out": nrm(ks[6], (N_A_LAYERS, RET_HEADS * RET_V_DIM, D), (RET_HEADS * RET_V_DIM) ** -0.5),
        "kv_norm_g": 1.0 + nrm(ks[7], (D,), 0.05),
        "kv_ada_w": nrm(ks[8], (D, 2 * D), 0.1 * D ** -0.5),
        "kv_ada_b": nrm(ks[9], (2 * D,), 0.01),
        "kv_w": nrm(ks[10], (D, 2 * SWA_KV_HEADS * SWA_HEAD_DIM), D ** -0.5),
        "swa_w_q": nrm(ks[11], (N_B_LAYERS, D, SWA_HEADS * SWA_HEAD_DIM), D ** -0.5),
        "swa_w_o": nrm(ks[12], (N_B_LAYERS, SWA_HEADS * SWA_HEAD_DIM, D), (SWA_HEADS * SWA_HEAD_DIM) ** -0.5),
        "swa_sinks": nrm(ks[13], (N_B_LAYERS, SWA_HEADS), 0.5),
        "rel_bias": nrm(ks[14], (REL_BUCKETS, SWA_HEADS), 0.5),
        "ffn_w_up": nrm(ks[15], (DEPTH, D, 2 * F), D ** -0.5),
        "ffn_conv_w": nrm(ks[16], (DEPTH, CONV_WIDTH, 2 * F), CONV_WIDTH ** -0.5),
        "ffn_conv_b": nrm(ks[17], (DEPTH, 2 * F), 0.01),
        "ffn_w_down": nrm(ks[18], (DEPTH, F, D), F ** -0.5),
    }

def reference(x, c, norm_g, ada_w, ada_b, ret_w_in, ret_w_out, kv_norm_g, kv_ada_w, kv_ada_b, kv_w,
              swa_w_q, swa_w_o, swa_sinks, rel_bias, ffn_w_up, ffn_conv_w, ffn_conv_b, ffn_w_down):
    S = x.shape[1]
    NB = S // BLOCK
    c_act = jax.nn.silu(c)
    bias, win = rel_bias_band(rel_bias)
    kpos = jnp.arange(NB)[:, None] * BLOCK - BLOCK + jnp.arange(2 * BLOCK)[None, :]
    mask = win[None] & (kpos >= 0)[:, None, :]
    k_band = None
    v_band = None
    for l in range(DEPTH):
        mod = c_act @ ada_w[l] + ada_b[l]
        sh_m, sc_m, gt_m, sh_f, sc_f, gt_f = jnp.split(mod, 6, axis=-1)
        h = adaln_in(x, norm_g[l, 0], sh_m, sc_m)
        if l < N_A_LAYERS:
            y = retention(h, ret_w_in[l], ret_w_out[l])
        else:
            i = l - N_A_LAYERS
            y = swa_sink_attention(h, swa_w_q[i], swa_w_o[i], swa_sinks[i], k_band, v_band, bias, mask)
        x = x + (1 + gt_m)[:, None, :] * rmsnorm(y, norm_g[l, 1])
        h = adaln_in(x, norm_g[l, 2], sh_f, sc_f)
        y = conv_ffn(h, ffn_w_up[l], ffn_conv_w[l], ffn_conv_b[l], ffn_w_down[l])
        x = x + (1 + gt_f)[:, None, :] * rmsnorm(y, norm_g[l, 3])
        if l == N_A_LAYERS - 1:
            kv_mod = c_act @ kv_ada_w + kv_ada_b
            kv_shift, kv_scale = jnp.split(kv_mod, 2, axis=-1)
            k_band, v_band = shared_kv(x, kv_norm_g, kv_shift, kv_scale, kv_w)
    return x


_drawn_inputs = setup_inputs


def setup_inputs(seed=0):
    import zlib

    import numpy as np

    out = dict(_drawn_inputs(seed))
    spreads = {}
    factors = {'swa_sinks': 8.0, 'ffn_conv_b': 4.106}
    for name, (base, spread) in spreads.items():
        noise = np.random.default_rng([zlib.crc32(name.encode()), seed]).standard_normal(out[name].shape)
        drawn = base * np.exp(spread * noise) if base else spread * noise
        out[name] = __import__('jax').numpy.asarray(drawn.astype(out[name].dtype))
    for name, factor in factors.items():
        out[name] = (out[name] * factor).astype(out[name].dtype)
    return out
```

```python
import math
from contextlib import ExitStack

import numpy as np

import concourse.bass as bass
from concourse import mybir

F32 = mybir.dt.float32
F32R = mybir.dt.float32r
ACT = mybir.ActivationFunctionType
ALU = mybir.AluOpType
AX = mybir.AxisListType

P = 128
D = 1024
S = 1024
KT = D // P
TT = S // P
HALF = 512
RH = 4
DK = D // RH
DV = 2 * D // RH
CH = 128
NC = S // CH
QH = 16
KVH = 4
HD = 64
BLK = 128
NB = S // BLK
FF = 2816
FT = FF // P
NG = FT // 2
EPS = 1e-6
NEG = -1e30
NVEC = 14

M_SH_M0, M_SC_M0, M_GT_M0, M_SH_F0, M_SC_F0, M_GT_F0, M_SH_KV, M_SC_KV = range(8)
M_SH_M1, M_SC_M1, M_GT_M1, M_SH_F1, M_SC_F1, M_GT_F1 = range(8, 14)

RET_SLOTS = 16
RET_UPS = 12
RET_ENTRIES = RET_SLOTS + 3 * KT
FFN_SLOTS = 6 * NG
KV_SLOTS = 4
SWA_SLOTS = 4
N_FFN0 = RET_SLOTS * RH
N_KV = N_FFN0 + FFN_SLOTS
N_SWA = N_KV + KV_SLOTS
N_FFN1 = N_SWA + SWA_SLOTS * KVH
N_SLOTS = N_FFN1 + FFN_SLOTS
U_FFN0 = RET_UPS * RH
U_KV = U_FFN0 + 4 * NG
U_SWA = U_KV + KV_SLOTS
U_FFN1 = U_SWA + 2 * KVH
ADA_STEPS = (0, 1, 4, 5, 12, 13)
RET_LOCAL = [j + 4 * sum(a < j for a in ADA_STEPS) for j in range(RET_SLOTS)]
D_FFN0 = 4 * RH
D_SWA = D_FFN0 + 2 * NG
D_FFN1 = D_SWA + 2 * KVH
E_CRIT = 2 * KT
E_LATER = NVEC * KT
N_ENTRIES = N_SLOTS + NVEC * KT

C_C = 0
C_ADAB = C_C + KT
C_NORM = C_ADAB + NVEC * KT
C_KVN = C_NORM + 8 * KT
C_CW = C_KVN + KT
C_CB = C_CW + 2 * 3 * 2 * FT
N_COLS = C_CB + 2 * 2 * FT

T_XI = 0
T_GINV = T_XI + RH * CH
T_ZETA = T_GINV + RH
T_GC = T_ZETA + RH
T_TRI = T_GC + RH
T_ID = T_TRI + CH
T_ONES = T_ID + P
N_TAB = T_ONES + P
BODY_UPS = (0, 1, 2, 3, 6, 7, 8, 9)
ML = 384


def trunk(nc, x_in, cols_d, stream_d, sinks_d, rel_d, rope_d, tab_d, hot_d, out):
    x_mid = [nc.dram_tensor(f"x_mid{i}", (S, D), F32).ap() for i in range(3)]
    k_dram = nc.dram_tensor("k_dram", (2 * P, S), F32).ap()
    bias_dram = nc.dram_tensor("bias_dram", (QH, P * ML), F32).ap()

    ctx = ExitStack()
    with ctx:
        offset = [nc.sbuf_base + (-nc.sbuf_base) % 32]

        def put(name, cols, dt=F32, at=None):
            where = offset[0] if at is None else at
            t = nc.alloc_sbuf_tensor_at(name, [P, cols], dt, offset=where)
            if at is None:
                offset[0] += 4 * cols + (-4 * cols) % 32
            return t, where

        H_hi = put("H_hi", KT * S, F32R)[0].ap().rearrange("p (k s) -> p k s", k=KT)
        H_lo = put("H_lo", KT * S, F32R)[0].ap().rearrange("p (k s) -> p k s", k=KT)
        y_acc = put("y_acc", TT * D)[0].ap().rearrange("p (t d) -> p t d", t=TT)
        g_t, g_at = put("G_hi", 4 * S, F32R)
        G_hi = g_t.ap().rearrange("p (f s) -> p f s", f=4)
        G_lo = put("G_lo", 4 * S, F32R)[0].ap().rearrange("p (f s) -> p f s", f=4)
        qk = put("qk", 4 * S, at=g_at)[0].ap().rearrange("p (f s) -> p f s", f=4)
        raw = put("raw", 2 * 1024)[0].ap().rearrange("p (r c) -> p r c", r=2)
        W_hi = put("W_hi", 2 * 1024, F32R)[0].ap().rearrange("p (r c) -> p r c", r=2)
        W_lo = put("W_lo", 2 * 1024, F32R)[0].ap().rearrange("p (r c) -> p r c", r=2)
        scr = put("scratch", 4 * 1024)[0].ap().rearrange("p (f s) -> p f s", f=4)
        state = put("state", 2 * 1024)[0].ap().rearrange("p (r c) -> p r c", r=2)
        cols = put("cols", N_COLS)[0].ap()
        tab = put("tab", N_TAB)[0].ap()
        mods = put("mods", NVEC * KT)[0].ap()
        amul = put("amul", KT)[0].ap()
        gvec = put("gvec", KT)[0].ap()
        ssq = put("ssq", 2 * TT)[0].ap()
        ms = put("ms", 2 * TT)[0].ap()
        rs = put("rs", 2 * TT)[0].ap()
        small = put("small", 64)[0].ap()
        shared_at = offset[0]
        rope = put("rope", 2 * S)[0].ap().rearrange("p (r s) -> p r s", r=2)
        acc = put("acc", 1024)[0].ap()
        v_sb = put("v_sb", 2 * DV)[0].ap().rearrange("p (r c) -> p r c", r=2)
        k_sb = put("k_sb", 2 * DK)[0].ap().rearrange("p (r c) -> p r c", r=2)
        sm = put("sm", 2 * CH)[0].ap().rearrange("p (r c) -> p r c", r=2)
        on = put("on", 2 * DV)[0].ap().rearrange("p (r c) -> p r c", r=2)
        assert offset[0] <= nc.sbuf_usable_end, offset[0]
        offset[0] = shared_at
        qT = put("qT", 2 * S)[0].ap().rearrange("p (f s) -> p f s", f=2)
        kd = state[:, 0, :]
        vtok = put("vtok", NB * KVH * HD)[0].ap().rearrange("p (b c) -> p b c", b=NB)
        vg = put("vg", NB * HD)[0].ap().rearrange("p (b c) -> p b c", b=NB)
        bias = state[:, 1, :].rearrange("p (h c) -> p h c", h=4)
        nsink = put("nsink", QH)[0].ap()
        stat = put("stat", 2 * 6 * 4)[0].ap().rearrange("p (r a h) -> p r a h", r=2, a=6)
        rel = put("rel", QH)[0].ap()
        hot = put("hot", ML)[0].ap()
        brow = put("brow", ML)[0].ap()
        assert offset[0] <= nc.sbuf_usable_end, offset[0]

        tri = tab[:, T_TRI:T_TRI + CH]
        ident = tab[:, T_ID:T_ID + P]
        ones = tab[:, T_ONES:T_ONES + P]
        pows = small[:, 0:1]
        bn6 = small[:, 8:14]
        mv = small[:, 16:20].rearrange("p (r c) -> p r c", r=2)
        ve = small[:, 20:22]
        rv = small[:, 22:24]

        ps = ctx.enter_context(nc.psum_tensor("ps", [P, 8 * 512], F32))

        def bank(b, n=1):
            return ps[:, 512 * b:512 * (b + n)]

        def sem(name):
            return ctx.enter_context(nc.semaphore(name))

        landed = [sem("landed0"), sem("landed1")]
        used = sem("used")
        w_hi = sem("w_hi")
        slot_done = sem("slot_done")
        u_free = sem("u_free")
        d_ready, d_free = sem("d_ready"), sem("d_free")
        consts, tabs_in, apart = sem("consts"), sem("tabs_in"), sem("apart")
        dve, rd_link, mx_link = sem("dve"), sem("rd_link"), sem("mx_link")
        a_bn, conv_mid = sem("a_bn"), sem("conv_mid")
        ada_red, ada_out = sem("ada_red"), sem("ada_out")
        y_zero = sem("y_zero")
        x_in_sem = [sem(f"x_in{i}") for i in range(4)]
        x_out_sem = [sem(f"x_out{i}") for i in range(4)]
        b_diag, b_row, b_gate = sem("b_diag"), sem("b_row"), sem("b_gate")
        b_sq, b_ms, b_rs, b_y, b_x, b_xn = (sem(n) for n in ("b_sq", "b_ms", "b_rs", "b_y", "b_x", "b_xn"))
        t_ready, h_tmp, h_hi, h_lo = sem("t_ready"), sem("h_tmp"), sem("h_hi"), sem("h_lo")
        rot_add = sem("rot_add")
        a_kt, a_vt, a_kv, a_s, a_m = (sem(n) for n in ("a_kt", "a_vt", "a_kv", "a_s", "a_m"))
        a_r, a_R, a_o, a_mv, a_ve, a_rs = (sem(n) for n in ("a_r", "a_R", "a_o", "a_mv", "a_ve", "a_rs"))
        a_on, a_ot, a_oe = (sem(n) for n in ("a_on", "a_ot", "a_oe"))
        g_sg, g_mul, g_hi, g_lo = (sem(n) for n in ("g_sg", "g_mul", "g_hi", "g_lo"))
        c_init = sem("c_init")
        kv_out, kv_vt, kv_vtok = sem("kv_out"), sem("kv_vt"), sem("kv_vtok")
        kd_in, bias_in, vg_in, ns_in = (sem(n) for n in ("kd_in", "bias_in", "vg_in", "ns_in"))
        r_set, r_in, r_mm, r_row, r_out = (sem(n) for n in ("r_set", "r_in", "r_mm", "r_row", "r_out"))
        s_qk, s_add, s_mx, s_ex = (sem(n) for n in ("s_qk", "s_add", "s_mx", "s_ex"))
        s_rd, s_p, s_pt, s_pa, s_pb = (sem(n) for n in ("s_rd", "s_p", "s_pt", "s_pa", "s_pb"))
        s_pv, s_oh, s_ol = (sem(n) for n in ("s_pv", "s_oh", "s_ol"))

        stream = stream_d.rearrange("e p c -> p e c")
        bias_rows = bass.AP(bias_dram.tensor, P - 1, [[P * ML, QH], [ML - 1, P], [1, 2 * BLK]])

        def column(where, k):
            return cols[:, where + k:where + k + 1]

        def norm_at(layer, i):
            return C_NORM + (layer * 4 + i) * KT

        BOUNDARIES = [
            (None, None, x_in, None, norm_at(0, 0), M_SC_M0, M_SH_M0),
            (norm_at(0, 1), M_GT_M0, x_in, x_mid[0], norm_at(0, 2), M_SC_F0, M_SH_F0),
            (norm_at(0, 3), M_GT_F0, x_mid[0], x_mid[1], C_KVN, M_SC_KV, M_SH_KV),
            (norm_at(1, 1), M_GT_M1, x_mid[1], x_mid[2], norm_at(1, 2), M_SC_F1, M_SH_F1),
            (norm_at(1, 3), M_GT_F1, x_mid[2], out, None, None, None),
        ]
        TURNS = [0, 1, 2, 4, 5]
        SQ_BEFORE = [0, TT, 3 * TT, 5 * TT, 7 * TT]

        def turn_counts(turn):
            return 2 * KT * turn

        def piece_landed(base, per, i, local):
            r = (base + local) % 2
            return r, 8 * per * i + 16 * ((base + local - r) // 2 + 1)

        block = ctx.enter_context(nc.Block())

        @block.sync
        def _(sp):
            for e in range(2):
                sp.dma_start(raw[:, e, :], stream[:, e, :]).then_inc(landed[e], 16)
            with sp.Fori(1, N_ENTRIES // 2) as i:
                for r in range(2):
                    sp.wait_ge(used, 2 * i + (r - 1))
                    sp.dma_start(raw[:, r:r + 1, :], stream[:, bass.ds(2 * i + r, 1), :]).then_inc(landed[r], 16)

        @block.tensor
        def _(pe):
            def up_slot(piece, u, j, hbase=None):
                w, pair = j % 2, j % 2
                pe.wait_ge(used, piece + 1)
                pe.wait_ge(u_free, u + 1)
                wh = W_hi[:, w, :].rearrange("p (k f) -> p k f", k=KT)
                wl = W_lo[:, w, :].rearrange("p (k f) -> p k f", k=KT)
                for half in range(2):
                    if hbase is not None:
                        pe.wait_ge(h_lo, hbase + KT * (half + 1))
                    o = bank(2 * pair + half)
                    tok = slice(HALF * half, HALF * (half + 1))
                    for k in range(KT):
                        nc.tensor.matmul(o, wh[:, k, :], H_hi[:, k, tok], start=(k == 0), stop=False)
                        nc.tensor.matmul(o, wh[:, k, :], H_lo[:, k, tok], start=False, stop=False)
                        last = nc.tensor.matmul(o, wl[:, k, :], H_hi[:, k, tok], start=False, stop=(k == KT - 1))
                last.then_inc(slot_done, 1)

            def down_slot(piece, dslot, w, f0):
                pe.wait_ge(used, piece + 1)
                wh = W_hi[:, w, :].rearrange("p (f c) -> p f c", f=2)
                wl = W_lo[:, w, :].rearrange("p (f c) -> p f c", f=2)
                for t in range(TT):
                    pe.wait_ge(d_free, TT * dslot + (t + 1))
                    o = bank(4 + t % 2)
                    tok = slice(P * t, P * (t + 1))
                    for f in range(2):
                        nc.tensor.matmul(o, G_hi[:, f0 + f, tok], wh[:, f, :], start=(f == 0), stop=False)
                        nc.tensor.matmul(o, G_hi[:, f0 + f, tok], wl[:, f, :], start=False, stop=False)
                        last = nc.tensor.matmul(o, G_lo[:, f0 + f, tok], wh[:, f, :], start=False, stop=(f == 1))
                    last.then_inc(d_ready if t < TT - 1 else slot_done, 1)

            def ada_reduce(v, piece):
                pe.wait_ge(used, piece + 1)
                if not isinstance(v, int) or v > 0:
                    pe.wait_ge(ada_out, v)
                for k in range(KT):
                    last = nc.tensor.matmul(bank(7)[:, k:k + 1], acc[:, P * k:P * (k + 1)], ones[:, 0:1],
                                            start=True, stop=True)
                last.then_inc(ada_red, 1)

            def turn(number, xn_base):
                for half in range(2):
                    pe.wait_ge(b_xn, xn_base + 4 * (half + 1))
                    for k in range(KT):
                        i = KT * half + k
                        if turn_counts(number) + i >= 2:
                            pe.wait_ge(h_tmp, turn_counts(number) + i - 1)
                        for t in range(4):
                            last = nc.tensor.transpose(bank(6 + k % 2)[:, P * t:P * (t + 1)],
                                                       y_acc[:, 4 * half + t, P * k:P * (k + 1)], ident)
                        last.then_inc(t_ready, 1)

            def gate_row(b, u_before):
                pe.wait_ge(b_diag, b)
                pe.wait_ge(u_free, u_before + 2)
                for half in range(2):
                    last = nc.tensor.matmul(bank(half), ones, state[:, 0, HALF * half:HALF * (half + 1)],
                                            start=True, stop=True)
                last.then_inc(b_row, 1)

            pe.wait_ge(tabs_in, 48)
            ada_reduce(0, KT - 1)
            ada_reduce(1, 2 * KT - 1)
            pe.wait_ge(ada_out, 2)
            turn(0, 0)

            def retention_chunk(h, c, part):
                tok = slice(CH * c, CH * (c + 1))
                if part == "turn":
                    for i in range(2):
                        last = nc.tensor.transpose(bank(3)[:, P * i:P * (i + 1)], qk[:, 2 + i, tok], ident)
                    last.then_inc(a_kt, 1)
                    for f in range(4):
                        last = nc.tensor.transpose(bank(6)[:, P * f:P * (f + 1)], scr[:, f, tok], ident)
                    last.then_inc(a_vt, 1)
                if part == "scores":
                    for i in range(2):
                        last = nc.tensor.matmul(bank(2)[:, 0:CH], qk[:, 2 + i, tok], qk[:, i, tok],
                                                start=(i == 0), stop=(i == 1))
                    last.then_inc(a_s, 1)
                if part == "state":
                    pe.wait_ge(a_kv, 16 * h + 2 * (c + 1))
                    if c > 0:
                        pe.wait_ge(a_R, 7 * h + c)
                    for i in range(2):
                        last = nc.tensor.matmul(bank(i), k_sb[:, c % 2, P * i:P * (i + 1)], v_sb[:, c % 2, :],
                                                start=True, stop=True)
                    last.then_inc(a_r, 1)
                if part == "out":
                    if c == NC - 1:
                        pe.wait_ge(a_kv, 16 * h + 2 * (c + 1))
                        pe.wait_ge(a_R, 7 * h + c)
                    pe.wait_ge(a_m, 8 * h + (c + 1))
                    o = bank(4 + c % 2)
                    last = nc.tensor.matmul(o, sm[:, c % 2, :], v_sb[:, c % 2, :], start=True, stop=(c == 0))
                    if c > 0:
                        for i in range(2):
                            last = nc.tensor.matmul(o, qk[:, i, tok], state[:, c % 2, DV * i:DV * (i + 1)],
                                                    start=False, stop=(i == 1))
                    last.then_inc(a_o, 1)
                if part == "back":
                    pe.wait_ge(a_on, 8 * h + (c + 1))
                    if c > 0:
                        pe.wait_ge(a_oe, 8 * h + c)
                    for f in range(4):
                        last = nc.tensor.transpose(bank(7)[:, P * f:P * (f + 1)],
                                                   on[:, c % 2, P * f:P * (f + 1)], ident)
                    last.then_inc(a_ot, 1)

            with pe.Fori(0, RH) as h:
                u0, v0 = RET_UPS * h, 3 * h + 2

                def piece(j):
                    return RET_ENTRIES * h + (E_CRIT + (1 + RET_LOCAL[j - 1] if j > 0 else 0))

                for j in range(8):
                    up_slot(piece(j), u0 + j, j, hbase=0 if j == 0 else None)
                    if j == 2:
                        ada_reduce(v0, piece(2) + 4)
                    if j == 6:
                        ada_reduce(v0 + 1, piece(6) + 4)
                pe.wait_ge(u_free, u0 + 10)
                pe.wait_ge(rot_add, 5 * h + 5)
                pe.wait_ge(d_free, 4 * TT * h + 2)
                pe.wait_ge(ada_out, v0 + 2)
                retention_chunk(h, 0, "turn")
                retention_chunk(h, 0, "scores")
                for c in range(NC):
                    if c < NC - 1:
                        retention_chunk(h, c, "state")
                    retention_chunk(h, c, "out")
                    if c < NC - 1:
                        retention_chunk(h, c + 1, "turn")
                        retention_chunk(h, c + 1, "scores")
                    if c > 0:
                        retention_chunk(h, c - 1, "back")
                retention_chunk(h, NC - 1, "back")
                for j in range(8, 12):
                    up_slot(piece(j), u0 + j, j)
                pe.wait_ge(a_oe, 8 * h + 8)
                for j in range(12, 16):
                    pe.wait_ge(g_lo, 4 * h + (2 if j < 14 else 4))
                    down_slot(piece(j), 4 * h + (j - 12), j % 2, 0 if j < 14 else 2)
                    if j == 14:
                        ada_reduce(v0 + 2, piece(14) + 4)

            pe.wait_ge(ada_out, NVEC)
            gate_row(1, U_FFN0)
            turn(1, TT)

            def ffn(n0, u0, d0, g0, hbase):
                def up_group(n, u, first=False):
                    for j in range(4):
                        up_slot(n + (E_LATER + j), u + j, j, hbase=hbase if first and j == 0 else None)

                def down_group(n, dslot, group, parity):
                    pe.wait_ge(g_lo, g0 + 2 * group + 2)
                    for j in range(2):
                        down_slot(n + (E_LATER + j), dslot + j, j % 2, 2 * parity)

                up_group(n0, u0, first=True)
                with pe.Fori(0, NG // 2) as i:
                    n, u, d = n0 + 4 + 12 * i, u0 + 4 + 8 * i, d0 + 4 * i
                    up_group(n, u)
                    down_group(n + 4, d, 2 * i, 0)
                    up_group(n + 6, u + 4)
                    down_group(n + 10, d + 2, 2 * i + 1, 1)
                down_group(n0 + FFN_SLOTS - 2, d0 + 2 * NG - 2, NG - 1, 0)

            ffn(N_FFN0, U_FFN0, D_FFN0, 4 * RH, turn_counts(1))
            gate_row(2, U_KV)
            turn(2, 2 * TT)

            for j in range(KV_SLOTS):
                up_slot(N_KV + E_LATER + j, U_KV + j, j, hbase=turn_counts(2) if j == 0 else None)
            pe.wait_ge(r_in, 32)
            pe.wait_ge(u_free, U_SWA + 2)
            nc.tensor.matmul(bank(0)[0:QH, 0:ML], rel[0:33, 0:QH], hot[0:33, :], start=True,
                             stop=True).then_inc(r_mm, 1)
            pe.wait_ge(h_tmp, turn_counts(3))
            for b in range(NB):
                if b >= 2:
                    pe.wait_ge(kv_vtok, b - 1)
                for f in range(2):
                    last = nc.tensor.transpose(bank(6 + b % 2)[:, P * f:P * (f + 1)],
                                               scr[:, 2 + f, BLK * b:BLK * (b + 1)], ident)
                last.then_inc(kv_vt, 1)
            pe.wait_ge(kv_vtok, NB)
            pe.wait_ge(r_row, 1)
            turn(3, 2 * TT)

            def scores(g, s):
                if s >= 2:
                    pe.wait_ge(s_add, NB * g + (s - 1))
                for half in range(2):
                    for i in range(2):
                        q = qT[HD * half:HD * (half + 1), i, BLK * s:BLK * (s + 1)]
                        lo = BLK * (s - 1) if s > 0 else 0
                        wide = 2 * BLK if s > 0 else BLK
                        o = bank(2 * (s % 2) + half)[:, 256 * i + 256 - wide:256 * i + 256]
                        last = nc.tensor.matmul(o, q, kd[HD * half:HD * (half + 1), lo:lo + wide],
                                                start=True, stop=True)
                last.then_inc(s_qk, 1)

            def probs_turned(g, s):
                pe.wait_ge(s_p, NB * g + (s + 1))
                if s >= 1:
                    pe.wait_ge(s_pb, NB * g + s)
                    if s >= 2:
                        pe.wait_ge(s_pa, (NB - 1) * g + (s - 1))
                for part in ((0, 1) if s > 0 else (1,)):
                    for hd in range(4):
                        last = nc.tensor.transpose(bank(6 + part)[:, P * hd:P * (hd + 1)],
                                                   scr[:, s % 2, 256 * hd + P * part:256 * hd + P * part + P],
                                                   ident)
                last.then_inc(s_pt, 1)

            def weighted(g, s):
                pe.wait_ge(s_pb, NB * g + (s + 1))
                if s > 0:
                    pe.wait_ge(s_pa, (NB - 1) * g + s)
                if s >= 2:
                    pe.wait_ge(s_ol, NB * g + (s - 1))
                parts = (0, 1) if s > 0 else (1,)
                for half in range(2):
                    o = bank(4 + s % 2)[HD * half:HD * (half + 1), 0:256]
                    for part in parts:
                        last = nc.tensor.matmul(o, vg[:, s - 1 + part, :],
                                                scr[:, 2 + s % 2, 512 * part + 256 * half:512 * part + 256 * half + 256],
                                                start=(part == parts[0]), stop=(part == parts[-1]))
                last.then_inc(s_pv, 1)

            with pe.Fori(0, KVH) as g:
                n0, u0 = N_SWA + SWA_SLOTS * g, U_SWA + 2 * g
                for j in range(2):
                    up_slot(n0 + (E_LATER + j), u0 + j, j, hbase=turn_counts(3) if j == 0 else None)
                pe.wait_ge(u_free, u0 + 4)
                pe.wait_ge(kd_in, 32 * g + 32)
                pe.wait_ge(vg_in, g + 1)
                pe.wait_ge(d_free, 2 * TT * g + (TT * D_SWA + 2))
                for s in range(NB + 3):
                    if s < NB:
                        scores(g, s)
                    if 2 <= s < NB + 2:
                        probs_turned(g, s - 2)
                    if s >= 3:
                        weighted(g, s - 3)
                pe.wait_ge(s_ol, NB * g + NB)
                for j in range(2):
                    down_slot(n0 + (E_LATER + 2 + j), 2 * g + (D_SWA + j), j % 2, 0)

            gate_row(3, U_FFN1)
            turn(4, 3 * TT)
            ffn(N_FFN1, U_FFN1, D_FFN1, 4 * RH + FT, turn_counts(4))
            gate_row(4, U_FFN1 + 4 * NG)

        @block.scalar
        def _(act):
            def split(n, piece, w):
                r, value = piece
                act.wait_ge(landed[r], value)
                act.wait_ge(slot_done, n + 1)
                nc.scalar.activation(W_hi[:, w, :], raw[:, r, :], ACT.Copy).then_inc(w_hi, 1)

            squares = [0]

            def sum_squares(src, col):
                if squares[0]:
                    act.wait_ge(b_sq, squares[0])
                squares[0] += 1
                nc.scalar.activation(bank(2, 2), src, ACT.Square, accum_out=ssq[:, col:col + 1]).then_inc(b_sq, 1)

            def load_x(b, t):
                act.dma_start(scr[:, t % 4, :],
                              BOUNDARIES[b][2][P * t:P * (t + 1), :]).then_inc(x_in_sem[t % 4], 16)

            def boundary(b):
                _, gate, _, x_new, norm_g, _, _ = BOUNDARIES[b]
                if gate is not None:
                    act.wait_ge(b_row, b)
                    nc.scalar.activation(state[:, 1, :], bank(0, 2), ACT.Copy).then_inc(b_gate, 1)
                    for t in range(TT):
                        sum_squares(y_acc[:, t, :], t)
                for t in range(TT + 2):
                    if t < TT:
                        if gate is None:
                            act.wait_ge(x_in_sem[t % 4], 16 * (t // 4 + 1))
                        else:
                            act.wait_ge(b_x, TT * (b - 1) + t + 1)
                        if x_new is not None:
                            act.dma_start(x_new[P * t:P * (t + 1), :],
                                          scr[:, t % 4, :]).then_inc(x_out_sem[t % 4], 16)
                        if norm_g is not None:
                            sum_squares(scr[:, t % 4, :], TT + t)
                    if 0 < t <= TT and norm_g is not None:
                        act.wait_ge(b_rs, SQ_BEFORE[b] + (TT if gate is not None else 0) + t)
                        nc.scalar.activation(y_acc[:, t - 1, :], scr[:, (t - 1) % 4, :], ACT.Copy,
                                             scale=rs[:, TT + t - 1:TT + t]).then_inc(b_xn, 1)
                    if 2 <= t < 6:
                        old = t - 2
                        if x_new is not None:
                            act.wait_ge(x_out_sem[old], 16 * (2 * (b - 1) + 1))
                        if norm_g is not None:
                            act.wait_ge(b_xn, TT * b + old + 1)
                        load_x(b, old + 4)

            def turn_hi(number):
                for i in range(2 * KT):
                    half, k = i // KT, i % KT
                    act.wait_ge(h_tmp, turn_counts(number) + i + 1)
                    nc.scalar.activation(H_hi[:, k, HALF * half:HALF * (half + 1)],
                                         state[:, 0, HALF * (i % 2):HALF * (i % 2 + 1)], ACT.Copy).then_inc(h_hi, 1)

            def stores_landed(b):
                for i in range(4):
                    act.wait_ge(x_out_sem[i], 16 * 2 * b)

            act.dma_start(cols, cols_d).then_inc(tabs_in, 16)
            act.dma_start(tab, tab_d).then_inc(tabs_in, 16)
            act.dma_start(rope, rope_d).then_inc(tabs_in, 16)
            for t in range(4):
                load_x(0, t)
            act.wait_ge(tabs_in, 48)
            nc.scalar.activation(small[:, 32:32 + KT], cols[:, C_C:C_C + KT], ACT.Silu).then_inc(consts, 1)
            boundary(0)
            turn_hi(0)
            split(0, piece_landed(E_CRIT, 0, 0, 0), 0)

            with act.Fori(0, RH) as h:
                n0 = RET_SLOTS * h
                for j in range(RET_SLOTS):
                    split(n0 + j + 1, piece_landed(E_CRIT + 1, RET_ENTRIES, h, RET_LOCAL[j]), (j + 1) % 2)
                    if 5 <= j <= 8:
                        f = j - 5
                        act.wait_ge(slot_done, n0 + j + 2)
                        if f == 0:
                            act.wait_ge(rot_add, 5 * h + 5)
                        nc.scalar.activation(scr[:, f, :], bank(2 * ((j - 1) % 2), 2), ACT.Copy).then_inc(u_free, 1)
                    if j == 8:
                        for c in range(NC + 1):
                            if c < NC:
                                act.wait_ge(a_kt, 8 * h + c + 1)
                                act.sem_inc(apart, 1)
                                nc.scalar.activation(k_sb[:, c % 2, :], bank(3)[:, 0:DK], ACT.Copy,
                                                     scale=tab[:, bass.ds(h + T_ZETA, 1)]).then_inc(a_kv, 1)
                                act.wait_ge(a_vt, 8 * h + c + 1)
                                nc.scalar.activation(v_sb[:, c % 2, :], bank(6), ACT.Copy).then_inc(a_kv, 1)
                            if c > 0:
                                act.wait_ge(a_ot, 8 * h + c)
                                nc.scalar.activation(scr[:, :, CH * (c - 1):CH * c],
                                                     bank(7).rearrange("p (f s) -> p f s", f=4),
                                                     ACT.Copy).then_inc(a_oe, 1)
                    if 9 <= j <= 12:
                        f = j - 9
                        act.wait_ge(slot_done, n0 + j + 2)
                        if f >= 2:
                            act.wait_ge(g_mul, 4 * h + f - 1)
                        nc.scalar.activation(state[:, f % 2, :], bank(2 * ((j - 1) % 2), 2),
                                             ACT.Silu).then_inc(u_free, 1)
                        act.wait_ge(g_mul, 4 * h + f + 1)
                        nc.scalar.activation(G_hi[:, f, :], scr[:, f, :], ACT.Copy).then_inc(g_hi, 1)

            def end_of_layer(b, g_count, d_slots):
                act.wait_ge(g_lo, g_count)
                for t in range(4):
                    load_x(b, t)
                act.wait_ge(d_free, TT * d_slots + 2)
                boundary(b)

            end_of_layer(1, 4 * RH, D_FFN0)
            turn_hi(1)
            stores_landed(1)

            def ffn(layer, n0, u0, g0):
                c0 = 2 * FT * layer

                def take(val, f, u, done, fp, buf, scratch_free=None):
                    act.wait_ge(slot_done, done)
                    if scratch_free is not None:
                        act.wait_ge(g_lo, scratch_free)
                    wcol = C_CW + (layer * 3 + 2) * 2 * FT + val * FT
                    bcol = C_CB + layer * 2 * FT + val * FT
                    act.sem_inc(apart, 1)
                    nc.scalar.activation(scr[:, 2 * fp + val, :], bank(2 * val, 2), ACT.Identity,
                                         bias=cols[:, bass.ds(f + bcol, 1)],
                                         scale=cols[:, bass.ds(f + wcol, 1)]).then_inc(c_init, 1)
                    if val:
                        act.wait_ge(u_free, u + 2)
                        nc.scalar.activation(scr[:, 2 * fp, :], scr[:, 2 * fp, :], ACT.Silu).then_inc(g_sg, 1)
                        act.wait_ge(g_mul, f + (g0 + 1))
                        nc.scalar.activation(G_hi[:, buf, :], scr[:, 2 * fp + 1, :], ACT.Copy).then_inc(g_hi, 1)

                for j in range(4):
                    split(n0 + j + 1, piece_landed(n0 + E_LATER + 1, 0, 0, j), (j + 1) % 2)
                    if j > 0:
                        take((j - 1) % 2, (j - 1) // 2, u0 + j - 1, n0 + j + 2, (j - 1) // 2, (j - 1) // 2)
                take(1, 1, u0 + 3, n0 + 6, 1, 1)
                with act.Fori(0, NG // 2) as i:
                    n, u = 12 * i + (n0 + 4), 8 * i + (u0 + 4)
                    for j in range(12):
                        split(n + (j + 1), piece_landed(n0 + 4 + E_LATER + 1, 12, i, j), (j + 1) % 2)
                        if j - 1 in BODY_UPS:
                            q = BODY_UPS.index(j - 1)
                            f = 4 * i + (2 + q // 2)
                            take(q % 2, f, u + q, n + (j + 2), (q // 2) % 2, (2 + q // 2) % 4,
                                 f + (g0 - 1) if q % 2 == 0 else None)
                for n in range(n0 + FFN_SLOTS - 2, n0 + FFN_SLOTS):
                    if n + 1 < N_SLOTS:
                        split(n + 1, piece_landed(n + 1 + E_LATER, 0, 0, 0), (n + 1) % 2)

            ffn(0, N_FFN0, U_FFN0, 4 * RH)
            end_of_layer(2, 4 * RH + FT, D_SWA)
            turn_hi(2)
            stores_landed(2)

            act.wait_ge(r_set, 1)
            act.dma_start(rel[0:32, :], rel_d).then_inc(r_in, 16)
            act.dma_start(hot[0:33, :], hot_d).then_inc(r_in, 16)
            for j in range(KV_SLOTS + 1):
                if j < KV_SLOTS:
                    split(N_KV + j + 1, piece_landed(N_KV + j + 1 + E_LATER, 0, 0, 0), (j + 1) % 2)
                if j > 0:
                    act.wait_ge(slot_done, N_KV + j + 2)
                    nc.scalar.activation(scr[:, j - 1, :], bank(2 * ((j - 1) % 2), 2), ACT.Copy).then_inc(u_free, 1)
            act.wait_ge(u_free, U_SWA + 2)
            for f in range(2):
                act.dma_start(k_dram[P * f:P * (f + 1), :], scr[:, f, :]).then_inc(kv_out, 16)
            act.wait_ge(r_mm, 1)
            nc.scalar.activation(brow[0:QH, :], bank(0)[0:QH, 0:ML], ACT.Copy).then_inc(r_row, 1)
            act.wait_ge(r_row, 1)
            act.dma_start(bias_dram.rearrange("h (r m) -> h r m", m=ML),
                          brow[0:QH, :].unsqueeze(1).to_broadcast([QH, P, ML])).then_inc(r_out, 16)
            for b in range(NB):
                act.wait_ge(kv_vt, b + 1)
                nc.scalar.activation(vtok[:, b, :], bank(6 + b % 2)[:, 0:2 * P], ACT.Copy).then_inc(kv_vtok, 1)
            turn_hi(3)
            act.wait_ge(h_lo, turn_counts(4))
            act.wait_ge(kv_out, 32)
            act.wait_ge(r_out, 16)

            with act.Fori(0, KVH) as g:
                n0 = SWA_SLOTS * g + N_SWA
                for half in range(2):
                    act.dma_start(kd[HD * half:HD * (half + 1), :], k_dram[bass.ds(HD * g, HD), :]).then_inc(kd_in, 16)
                act.dma_start(bias, bias_rows[bass.ds(4 * g, 4), :, :].rearrange("h p c -> p h c")).then_inc(bias_in, 16)
                for j in range(3):
                    split(n0 + (j + 1), piece_landed(N_SWA + 1 + E_LATER, SWA_SLOTS, g, j), (j + 1) % 2)
                    if j > 0:
                        act.wait_ge(slot_done, n0 + (j + 2))
                        nc.scalar.activation(qT[:, j - 1, :], bank(2 * (j - 1), 2), ACT.Copy,
                                             scale=HD ** -0.5).then_inc(u_free, 1)
                for s in range(NB + 4):
                    if s < NB:
                        act.wait_ge(s_mx, NB * g + s + 1)
                        w0 = 0 if s > 0 else BLK
                        for hd in range(4):
                            e = scr[:, s % 2, 256 * hd + w0:256 * hd + 256]
                            nc.scalar.activation(e, e, ACT.Exp, bias=stat[:, s % 2, 1, hd:hd + 1],
                                                 accum_out=stat[:, s % 2, 2, hd:hd + 1])
                        nc.scalar.activation(stat[:, s % 2, 3, :], stat[:, s % 2, 4, :], ACT.Exp).then_inc(s_ex, 1)
                    if 3 <= s < NB + 2:
                        act.wait_ge(s_pt, NB * g + (s - 1))
                        nc.scalar.activation(scr[:, 2 + s % 2, 0:512], bank(6), ACT.Copy).then_inc(s_pa, 1)
                    if s >= 4:
                        b = s - 4
                        act.wait_ge(s_pv, NB * g + (b + 1))
                        nc.scalar.activation(G_hi[:, 0:2, BLK * b:BLK * (b + 1)],
                                             bank(4 + b % 2)[:, 0:256].rearrange("p (f s) -> p f s", f=2),
                                             ACT.Copy).then_inc(s_oh, 1)
                split(n0 + 4, piece_landed(N_SWA + 1 + E_LATER, SWA_SLOTS, g, 3), 0)

            act.wait_ge(s_ol, NB * KVH)
            end_of_layer(3, 4 * RH + FT, D_FFN1)
            turn_hi(4)
            stores_landed(3)
            ffn(1, N_FFN1, U_FFN1, 4 * RH + FT)
            end_of_layer(4, 4 * RH + 2 * FT, D_FFN1 + 2 * NG)
            stores_landed(4)

        @block.vector
        def _(v):
            links = [0]

            def link(ins):
                links[0] += 1
                ins.then_inc(dve, 1)
                v.wait_ge(dve, links[0])

            def split(n, r, w):
                v.wait_ge(w_hi, n + 1)
                nc.vector.tensor_tensor(W_lo[:, w, :], raw[:, r, :], W_hi[:, w, :].bitcast(F32),
                                        ALU.subtract).then_inc(used, 1)

            def ada_unit(k, piece, before):
                r, value = piece
                v.wait_ge(landed[r], value)
                c_k = small[:, 32 + k:33 + k]
                if k == 0:
                    nc.vector.tensor_scalar(acc, raw[:, r, :], c_k, None, ALU.mult).then_inc(used, 1)
                else:
                    v.wait_ge(used, before)
                    nc.vector.scalar_tensor_tensor(acc, raw[:, r, :], c_k, acc, ALU.mult, ALU.add).then_inc(used, 1)

            def ada_column(vec):
                v.wait_ge(ada_red, vec + 1)
                nc.vector.tensor_tensor(mods[:, bass.ds(KT * vec, KT)], bank(7)[:, 0:KT],
                                        cols[:, bass.ds(KT * vec + C_ADAB, KT)], ALU.add).then_inc(ada_out, 1)

            def gain(dst, scale, g_col):
                return nc.vector.scalar_tensor_tensor(dst, mods[:, KT * scale:KT * (scale + 1)], 1.0,
                                                      cols[:, g_col:g_col + KT], ALU.add, ALU.mult)

            def boundary(b):
                norm_y, gate, _, _, norm_g, scale, _ = BOUNDARIES[b]
                if norm_g is not None:
                    link(gain(amul, scale, norm_g))
                if gate is None:
                    return
                link(gain(gvec, gate, norm_y))
                if b == 1:
                    v.wait_ge(g_mul, 4 * RH)
                else:
                    v.wait_ge(h_lo, turn_counts(TURNS[b]))
                nc.vector.tensor_tensor(state[:, 0, :].rearrange("p (k f) -> p k f", k=KT),
                                        ident.unsqueeze(1).to_broadcast([P, KT, P]),
                                        gvec.unsqueeze(2).to_broadcast([P, KT, P]), ALU.mult).then_inc(b_diag, 1)
                v.wait_ge(b_gate, b)
                for t in range(TT):
                    v.wait_ge(b_rs, SQ_BEFORE[b] + t + 1)
                    nc.vector.scalar_tensor_tensor(y_acc[:, t, :], y_acc[:, t, :], rs[:, t:t + 1],
                                                   state[:, 1, :], ALU.mult, ALU.mult).then_inc(b_y, 1)
                    v.wait_ge(b_y, TT * (b - 1) + t + 1)
                    v.wait_ge(x_in_sem[t % 4], 16 * (2 * b + t // 4 + 1))
                    nc.vector.tensor_tensor(scr[:, t % 4, :], scr[:, t % 4, :], y_acc[:, t, :],
                                            ALU.add).then_inc(b_x, 1)

            def turn_tmp(number, shift):
                for i in range(2 * KT):
                    k = i % KT
                    v.wait_ge(t_ready, turn_counts(number) + i + 1)
                    if i >= 2 or number > 0:
                        v.wait_ge(h_lo, turn_counts(number) + i - 1)
                    nc.vector.tensor_scalar(state[:, 0, HALF * (i % 2):HALF * (i % 2 + 1)], bank(6 + k % 2),
                                            amul[:, k:k + 1], mods[:, KT * shift + k:KT * shift + k + 1],
                                            ALU.mult, ALU.add).then_inc(h_tmp, 1)

            def add_tile(t, half, ready, value):
                v.wait_ge(ready, value)
                y = y_acc[:, t, HALF * half:HALF * (half + 1)]
                nc.vector.tensor_tensor(y, bank(4 + t % 2), y, ALU.add).then_inc(d_free, 1)

            def down_step(n, dslot, half, others):
                others = list(others)
                for t in range(TT):
                    if t < TT - 1:
                        add_tile(t, half, d_ready, (TT - 1) * dslot + (t + 1))
                    else:
                        add_tile(t, half, slot_done, n + 3)
                    if others:
                        others.pop(0)()

            v.wait_ge(consts, 1)
            for vec in range(2):
                for k in range(KT):
                    ada_unit(k, piece_landed(KT * vec + k, 0, 0, 0), KT * vec + k)
                v.wait_ge(ada_red, vec + 1)
                link(nc.vector.tensor_tensor(mods[:, KT * vec:KT * (vec + 1)], bank(7)[:, 0:KT],
                                             cols[:, C_ADAB + KT * vec:C_ADAB + KT * (vec + 1)], ALU.add))
                v.sem_inc(ada_out, 1)
            boundary(0)
            turn_tmp(0, M_SH_M0)
            split(0, 0, 0)

            with v.Fori(0, RH) as h:
                n0, u0, vec0 = RET_SLOTS * h, RET_UPS * h, 3 * h + 2
                for j in range(RET_SLOTS):
                    local = RET_LOCAL[j]
                    if j < 12:
                        split(n0 + (j + 1), (E_CRIT + 1 + local) % 2, (j + 1) % 2)
                    else:
                        down_step(n0 + j, 4 * h + (j - 12), j % 2,
                                  [lambda: split(n0 + (j + 1), (E_CRIT + 1 + local) % 2, (j + 1) % 2)])
                    if 1 <= j <= 4:
                        i, part = (j - 1) // 2, (j - 1) % 2
                        v.wait_ge(slot_done, n0 + (j + 2))
                        x = bank(2 * part, 2)
                        sin_to, cos_to = scr[:, 2 * i + part, :], qk[:, 2 * i + part, :]
                        nc.vector.tensor_tensor(cos_to, x, rope[:, 0, :], ALU.mult)
                        nc.vector.tensor_tensor(sin_to, x, rope[:, 1, :], ALU.mult).then_inc(u_free, 1)
                    if j == 4:
                        ada_column(vec0)
                    if j == 8:
                        ada_column(vec0 + 1)
                        for c in range(NC):
                            v.wait_ge(a_s, 8 * h + (c + 1))
                            nc.vector.scalar_tensor_tensor(sm[:, c % 2, :], bank(2)[:, 0:CH],
                                                           tab[:, bass.ds(h + T_GINV, 1)], tri,
                                                           ALU.mult, ALU.mult).then_inc(a_m, 1)
                            if c < NC - 1:
                                v.wait_ge(a_r, 7 * h + (c + 1))
                                new = state[:, (c + 1) % 2, :]
                                if c == 0:
                                    nc.vector.tensor_copy(new, bank(0, 2)).then_inc(a_R, 1)
                                else:
                                    v.wait_ge(a_R, 7 * h + c)
                                    nc.vector.scalar_tensor_tensor(new, state[:, c % 2, :],
                                                                   tab[:, bass.ds(h + T_GC, 1)], bank(0, 2),
                                                                   ALU.mult, ALU.add).then_inc(a_R, 1)
                            v.wait_ge(a_o, 8 * h + (c + 1))
                            nc.vector.bn_stats(bn6, bank(4 + c % 2)).then_inc(a_bn, 1)
                            v.wait_ge(a_bn, 8 * h + (c + 1))
                            v.sem_inc(apart, 1)
                            nc.vector.bn_aggr(mv[:, c % 2, :], bn6).then_inc(a_mv, 1)
                            v.wait_ge(a_rs, 8 * h + (c + 1))
                            nc.vector.tensor_scalar(on[:, c % 2, :], bank(4 + c % 2), mv[:, c % 2, 0:1],
                                                    rv[:, c % 2:c % 2 + 1], ALU.subtract, ALU.mult).then_inc(a_on, 1)
                    if j in ADA_STEPS:
                        first = ADA_STEPS.index(j) % 2 * 4
                        for k in range(4):
                            at = local + 1 + k
                            ada_unit(first + k, piece_landed(E_CRIT + 1, RET_ENTRIES, h, at),
                                     RET_ENTRIES * h + (E_CRIT + 1 + at))
                    if j == 15:
                        ada_column(vec0 + 2)

            boundary(1)
            turn_tmp(1, M_SH_F0)

            def ffn(layer, n0, u0, d0, zero):
                c0 = 2 * FT * layer

                def conv(val, f, q, fp):
                    dst, src = scr[:, 2 * fp + val, :], bank(2 * val, 2)
                    col = C_CW + layer * 3 * 2 * FT + val * FT

                    def one_back():
                        v.wait_ge(c_init, q + (c0 + 1))
                        nc.vector.scalar_tensor_tensor(dst[:, 1:], src[:, :S - 1],
                                                       cols[:, bass.ds(f + (col + 2 * FT), 1)], dst[:, 1:],
                                                       ALU.mult, ALU.add).then_inc(conv_mid, 1)

                    def two_back():
                        v.wait_ge(conv_mid, q + (c0 + 1))
                        nc.vector.scalar_tensor_tensor(dst[:, 2:], src[:, :S - 2],
                                                       cols[:, bass.ds(f + col, 1)], dst[:, 2:],
                                                       ALU.mult, ALU.add).then_inc(u_free, 1)

                    return [one_back, two_back]

                def run(steps):
                    for step in steps:
                        step()

                for j in range(4):
                    split(n0 + j + 1, (j + 1) % 2, (j + 1) % 2)
                    if j > 0:
                        run(conv((j - 1) % 2, (j - 1) // 2, j - 1, (j - 1) // 2))
                run(conv(1, 1, 3, 1))
                v.wait_ge(y_zero, zero)
                with v.Fori(0, NG // 2) as i:
                    n = 12 * i + (n0 + 4)
                    for j in range(12):
                        work = [lambda: split(n + (j + 1), (j + 1) % 2, (j + 1) % 2)]
                        if j - 1 in BODY_UPS:
                            q = BODY_UPS.index(j - 1)
                            work += conv(q % 2, 4 * i + (2 + q // 2), 8 * i + (4 + q), (q // 2) % 2)
                        if j in BODY_UPS:
                            run(work)
                        else:
                            dslot = 4 * i + (d0 + (j - 4 if j < 6 else j - 8))
                            down_step(n + j, dslot, j % 2, work)
                for j in range(2):
                    n = n0 + FFN_SLOTS - 2 + j
                    down_step(n, d0 + 2 * NG - 2 + j, j,
                              [lambda: split(n + 1, (n + 1) % 2, (n + 1) % 2)] if n + 1 < N_SLOTS else [])

            ffn(0, N_FFN0, U_FFN0, D_FFN0, 2)
            boundary(2)
            turn_tmp(2, M_SH_KV)

            for j in range(KV_SLOTS):
                split(N_KV + j + 1, (j + 1) % 2, (j + 1) % 2)
            link(gain(amul, M_SC_M1, norm_at(1, 0)))
            turn_tmp(3, M_SH_M1)
            v.wait_ge(ns_in, 16)
            link(nc.vector.tensor_scalar(nsink, nsink, -1.0, None, ALU.mult))
            v.wait_ge(y_zero, 3)

            with v.Fori(0, KVH) as g:
                n0 = SWA_SLOTS * g + N_SWA
                for j in range(3):
                    split(n0 + (j + 1), (j + 1) % 2, (j + 1) % 2)
                v.wait_ge(bias_in, 16 * g + 16)
                for s in range(NB + 4):
                    if s < NB:
                        r, w0 = s % 2, (0 if s > 0 else BLK)
                        st = scr[:, r, :].rearrange("p (h c) -> p h c", h=4)[:, :, w0:]
                        v.wait_ge(s_qk, NB * g + (s + 1))
                        if s >= 2:
                            v.wait_ge(s_pt, NB * g + (s - 1))
                        nc.vector.tensor_tensor(st, bank(2 * r, 2).rearrange("p (h c) -> p h c", h=4)[:, :, w0:],
                                                bias[:, :, w0:], ALU.add).then_inc(s_add, 1)
                        v.wait_ge(s_add, NB * g + (s + 1))
                        nc.vector.tensor_reduce(stat[:, r, 0, :], st, AX.X, ALU.max, negate=True).then_inc(mx_link, 1)
                        v.wait_ge(mx_link, 2 * NB * g + (2 * s + 1))
                        ns = nsink[:, bass.ds(4 * g, 4)]
                        nc.vector.tensor_tensor(stat[:, r, 1, :], stat[:, r, 0, :], ns, ALU.min).then_inc(mx_link, 1)
                        v.wait_ge(mx_link, 2 * NB * g + (2 * s + 2))
                        nc.vector.tensor_tensor(stat[:, r, 4, :], stat[:, r, 1, :], ns, ALU.subtract).then_inc(s_mx, 1)
                    if 1 <= s <= NB:
                        r = (s - 1) % 2
                        v.wait_ge(s_ex, NB * g + s)
                        nc.vector.tensor_tensor(stat[:, r, 5, :], stat[:, r, 2, :], stat[:, r, 3, :],
                                                ALU.add).then_inc(rd_link, 1)
                        v.wait_ge(rd_link, NB * g + s)
                        nc.vector.reciprocal(stat[:, r, 5, :], stat[:, r, 5, :]).then_inc(s_rd, 1)
                    if 2 <= s < NB + 2:
                        v.wait_ge(s_pt, NB * g + (s - 1))
                        nc.vector.tensor_copy(scr[:, 2 + s % 2, 512:1024], bank(7)).then_inc(s_pb, 1)
                    if s >= 4:
                        b = s - 4
                        v.wait_ge(s_oh, NB * g + (b + 1))
                        o = slice(BLK * b, BLK * (b + 1))
                        nc.vector.tensor_tensor(G_lo[:, 0:2, o],
                                                bank(4 + b % 2)[:, 0:256].rearrange("p (f s) -> p f s", f=2),
                                                G_hi[:, 0:2, o].bitcast(F32), ALU.subtract).then_inc(s_ol, 1)
                for j in range(2):
                    down_step(n0 + (2 + j), 2 * g + (D_SWA + j), j,
                              [lambda: split(n0 + 4, 0, 0)] if j == 1 else [])

            boundary(3)
            turn_tmp(4, M_SH_F1)
            ffn(1, N_FFN1, U_FFN1, D_FFN1, 4)
            boundary(4)

        @block.gpsimd
        def _(gp):
            def root_mean_squares(b):
                both = [0] if b in (0, 4) else [0, 1]
                count = SQ_BEFORE[b]
                for part in both:
                    for t in range(TT):
                        col = t + (TT if b == 0 or part == 1 else 0)
                        count += 1
                        gp.wait_ge(b_sq, count)
                        gp.tensor_scalar(ms[:, col:col + 1], ssq[:, col:col + 1], 1.0 / D, EPS,
                                         ALU.mult, ALU.add).then_inc(b_ms, 1)
                        gp.wait_ge(b_ms, count)
                        gp.tensor_tensor(rs[:, col:col + 1], ms[:, col:col + 1], pows, ALU.pow).then_inc(b_rs, 1)

            def turn_lo(number, clear=True):
                for i in range(2 * KT):
                    half, k = i // KT, i % KT
                    tok = slice(HALF * half, HALF * (half + 1))
                    gp.wait_ge(h_hi, turn_counts(number) + i + 1)
                    gp.tensor_tensor(H_lo[:, k, tok], state[:, 0, HALF * (i % 2):HALF * (i % 2 + 1)],
                                     H_hi[:, k, tok].bitcast(F32), ALU.subtract).then_inc(h_lo, 1)
                if clear:
                    gp.memset(y_acc, 0.0).then_inc(y_zero, 1)

            gp.memset(pows, -0.5).then_inc(slot_done, 2)
            gp.memset(small[:, 1:2], 0.0).then_inc(u_free, 2)
            gp.memset(small[:, 2:3], 0.0).then_inc(d_free, 2)
            gp.wait_ge(slot_done, 2)
            root_mean_squares(0)
            turn_lo(0)

            with gp.Fori(0, RH) as h:
                u0 = RET_UPS * h
                for i in range(2):
                    gp.wait_ge(u_free, u0 + (2 * i + 4))
                    a, b = qk[:, 2 * i, :], qk[:, 2 * i + 1, :]
                    gp.tensor_tensor(a, a, scr[:, 2 * i + 1, :], ALU.subtract).then_inc(rot_add, 1)
                    gp.tensor_tensor(b, b, scr[:, 2 * i, :], ALU.add).then_inc(rot_add, 1)
                    if i == 0:
                        gp.wait_ge(rot_add, 5 * h + 2)
                        both = qk[:, 0:2, :].rearrange("p i (c s) -> p (i c) s", c=NC)
                        xi = tab[:, bass.ds(CH * h + T_XI, CH)]
                        gp.tensor_tensor(both, both, xi.unsqueeze(1).to_broadcast([P, 2 * NC, CH]),
                                         ALU.mult).then_inc(rot_add, 1)
                for c in range(NC):
                    gp.wait_ge(a_mv, 8 * h + (c + 1))
                    gp.sem_inc(apart, 1)
                    gp.tensor_scalar(ve[:, c % 2:c % 2 + 1], mv[:, c % 2, 1:2], EPS, None, ALU.add).then_inc(a_ve, 1)
                    gp.wait_ge(a_ve, 8 * h + (c + 1))
                    gp.tensor_tensor(rv[:, c % 2:c % 2 + 1], ve[:, c % 2:c % 2 + 1], pows, ALU.pow).then_inc(a_rs, 1)
                for f in range(4):
                    gp.wait_ge(u_free, u0 + (8 + f + 3))
                    gp.tensor_tensor(scr[:, f, :], scr[:, f, :], state[:, f % 2, :], ALU.mult).then_inc(g_mul, 1)
                    gp.wait_ge(g_hi, 4 * h + (f + 1))
                    gp.tensor_tensor(G_lo[:, f, :], scr[:, f, :], G_hi[:, f, :].bitcast(F32),
                                     ALU.subtract).then_inc(g_lo, 1)

            root_mean_squares(1)
            turn_lo(1)

            def ffn(layer, u0, g0):
                def tile(f, u, fp, buf):
                    gp.wait_ge(g_sg, f + (FT * layer + 1))
                    gp.wait_ge(u_free, u + 3)
                    m = scr[:, 2 * fp + 1, :]
                    gp.tensor_tensor(m, m, scr[:, 2 * fp, :], ALU.mult).then_inc(g_mul, 1)
                    gp.wait_ge(g_hi, f + (g0 + 1))
                    gp.tensor_tensor(G_lo[:, buf, :], m, G_hi[:, buf, :].bitcast(F32),
                                     ALU.subtract).then_inc(g_lo, 1)

                for f in range(2):
                    tile(f, u0 + 2 * f + 1, f, f)
                with gp.Fori(0, NG // 2) as i:
                    for q in range(4):
                        tile(4 * i + (2 + q), 8 * i + (u0 + 4 + 2 * q + 1), q % 2, (2 + q) % 4)

            ffn(0, U_FFN0, 4 * RH)
            root_mean_squares(2)
            turn_lo(2, clear=False)
            gp.memset(rel[0:64, :], 1.0).then_inc(r_set, 1)
            gp.dma_start(nsink, sinks_d.to_broadcast([P, QH])).then_inc(ns_in, 16)
            turn_lo(3)
            gp.wait_ge(kv_vtok, NB)

            with gp.Fori(0, KVH) as g:
                n0 = SWA_SLOTS * g + N_SWA
                gp.wait_ge(slot_done, n0 + 2)
                gp.tensor_copy(vg, vtok[:, :, bass.ds(HD * g, HD)]).then_inc(vg_in, 1)
                for s in range(NB):
                    gp.wait_ge(s_rd, NB * g + (s + 1))
                    w0 = 0 if s > 0 else BLK
                    e = scr[:, s % 2, :].rearrange("p (h c) -> p h c", h=4)[:, :, w0:]
                    gp.tensor_tensor(e, e, stat[:, s % 2, 5, :].unsqueeze(2).to_broadcast([P, 4, 256 - w0]),
                                     ALU.mult).then_inc(s_p, 1)

            root_mean_squares(3)
            turn_lo(4)
            ffn(1, U_FFN1, 4 * RH + FT)
            root_mean_squares(4)


def _tables():
    f4 = np.float32
    inv = f4(10000.0) ** (-np.arange(P, dtype=f4) / f4(P))
    ang = (np.arange(S, dtype=f4)[None, :] * inv[:, None]).astype(f4)
    rope = np.stack([np.cos(ang), np.sin(ang)], 1).astype(f4).reshape(P, 2 * S)
    gamma = 1.0 - 2.0 ** (-5.0 - np.arange(RH))
    i = np.arange(CH)
    tab = np.zeros((P, N_TAB))
    tab[:, T_XI:T_XI + RH * CH] = (gamma[:, None] ** (i + 1)).reshape(1, -1)
    tab[:, T_GINV:T_GINV + RH] = gamma[None, :] ** -(i[:, None] + 1.0) * DK ** -0.5
    tab[:, T_ZETA:T_ZETA + RH] = gamma[None, :] ** (CH - 1.0 - i[:, None]) * DK ** -0.5
    tab[:, T_GC:T_GC + RH] = gamma[None, :] ** float(CH)
    tab[:, T_TRI:T_TRI + CH] = i[None, :] >= i[:, None]
    tab[:, T_ID:T_ID + P] = np.eye(P)
    tab[:, T_ONES:T_ONES + P] = 1.0
    n = np.arange(BLK)
    large = 16 + (np.log(np.maximum(n, 1).astype(f4) / 16) / math.log(128 / 16) * 16).astype(np.int32)
    bucket = np.where(n < 16, n, np.minimum(large, 31))
    hot = np.zeros((33, ML))
    for w in range(ML):
        dist = 255 - w
        if 0 <= dist < BLK:
            hot[bucket[dist], w] = 1.0
        else:
            hot[32, w] = NEG
    return rope, tab.astype(f4), hot.astype(f4)


def _up(w, f):
    return w[:, f].reshape(KT, P, P).transpose(1, 0, 2).reshape(P, 1024)


def _down(w, f, half):
    return w[P * f:P * (f + 2), HALF * half:HALF * (half + 1)].reshape(2, P, HALF).transpose(1, 0, 2).reshape(P, 1024)


def _ada(w, v, k):
    return w[P * k:P * (k + 1), D * v:D * (v + 1)]


def _stream(a):
    vectors = [(a["ada_w"][0], v) for v in range(6)] + [(a["kv_ada_w"], v) for v in range(2)] \
        + [(a["ada_w"][1], v) for v in range(6)]
    win, wout = a["ret_w_in"][0], a["ret_w_out"][0]
    slots = []
    for h in range(RH):
        starts = [DK * h + P * i for i in range(2)] + [D + DK * h + P * i for i in range(2)] \
            + [2 * D + DV * h + P * i for i in range(4)] + [4 * D + DV * h + P * i for i in range(4)]
        slots += [_up(win, slice(s, s + P)) for s in starts]
        slots += [_down(wout, 4 * h + 2 * g, half) for g in range(2) for half in range(2)]

    def ffn(layer):
        up, down, made = a["ffn_w_up"][layer], a["ffn_w_down"][layer], []

        def ups(g):
            return [_up(up, slice(P * (f + FT * val), P * (f + FT * val + 1))) for f in (2 * g, 2 * g + 1)
                    for val in range(2)]

        def downs(g):
            return [_down(down, 2 * g, half) for half in range(2)]

        made += ups(0)
        for g in range(1, NG):
            made += ups(g) + downs(g - 1)
        return made + downs(NG - 1)

    slots += ffn(0)
    slots += [_up(a["kv_w"], slice(P * f, P * (f + 1))) for f in range(4)]
    wq, wo = a["swa_w_q"][0], a["swa_w_o"][0]
    for g in range(KVH):
        order = [np.r_[HD * (4 * g + i):HD * (4 * g + i + 1), HD * (4 * g + 2 + i):HD * (4 * g + 3 + i)]
                 for i in range(2)]
        slots += [_up(wq, o) for o in order]
        rows = wo[np.concatenate(order)]
        slots += [_down(rows, 0, half) for half in range(2)]
    slots += ffn(1)
    assert len(slots) == N_SLOTS

    units = [_ada(w, v, k) for w, v in vectors for k in range(KT)]
    pieces = units[:E_CRIT] + [slots[0]]
    units, slots = units[E_CRIT:], slots[1:]
    for _ in range(RH):
        for j in range(RET_SLOTS):
            pieces.append(slots.pop(0))
            if j in ADA_STEPS:
                pieces += units[:4]
                units = units[4:]
    pieces += slots
    assert len(pieces) == N_ENTRIES and not units
    return np.stack(pieces)


def _columns(a):
    vectors = [a["c"].reshape(-1), a["ada_b"][0], a["kv_ada_b"], a["ada_b"][1], a["norm_g"].reshape(-1), a["kv_norm_g"],
               a["ffn_conv_w"].reshape(-1), a["ffn_conv_b"].reshape(-1)]
    return np.ascontiguousarray(np.concatenate(vectors).reshape(N_COLS, P).T)


def kernel(**inputs):
    import concourse.bacc as bacc
    from concourse.bass_utils import run_bass_kernel_spmd

    a = {name: np.asarray(value) for name, value in inputs.items()}
    rope, tab, hot = _tables()
    arrays = {
        "x": np.ascontiguousarray(a["x"][0]), "cols": _columns(a), "stream": _stream(a),
        "sinks": a["swa_sinks"], "rel": a["rel_bias"], "rope": rope, "tab": tab, "hot": hot,
    }
    nc = bacc.Bacc("TRN2", target_bir_lowering=False, num_devices=1)
    args = [nc.dram_tensor(f"in_{name}", value.shape, mybir.dt.from_np(value.dtype), kind="ExternalInput").ap()
            for name, value in arrays.items()]
    out = nc.dram_tensor("out", (S, D), F32, kind="ExternalOutput").ap()
    trunk(nc, *args, out)
    run = run_bass_kernel_spmd(nc, [{f"in_{name}": value for name, value in arrays.items()}], core_ids=[0])
    return run.results[0]["out"].reshape(1, S, D)
```

```python
import math
from contextlib import ExitStack

import numpy as np

import concourse.bass as bass
from concourse import mybir

F32 = mybir.dt.float32
F32R = mybir.dt.float32r
ACT = mybir.ActivationFunctionType
ALU = mybir.AluOpType
AX = mybir.AxisListType

P = 128
D = 1024
S = 1024
KT = D // P
TT = S // P
HALF = 512
RH = 4
DK = D // RH
DV = 2 * D // RH
CH = 128
NC = S // CH
QH = 16
KVH = 4
HD = 64
BLK = 128
NB = S // BLK
FF = 2816
FT = FF // P
NG = FT // 2
EPS = 1e-6
NEG = -1e30
NVEC = 14

M_SH_M0, M_SC_M0, M_GT_M0, M_SH_F0, M_SC_F0, M_GT_F0, M_SH_KV, M_SC_KV = range(8)
M_SH_M1, M_SC_M1, M_GT_M1, M_SH_F1, M_SC_F1, M_GT_F1 = range(8, 14)

RET_SLOTS = 16
RET_UPS = 8
RET_ENTRIES = RET_SLOTS + 3 * KT
FFN_SLOTS = 6 * NG
KV_SLOTS = 4
SWA_SLOTS = 4
N_FFN0 = RET_SLOTS * RH
N_KV = N_FFN0 + FFN_SLOTS
N_SWA = N_KV + KV_SLOTS
N_FFN1 = N_SWA + SWA_SLOTS * KVH
N_SLOTS = N_FFN1 + FFN_SLOTS
U_FFN0 = RET_UPS * RH
U_KV = U_FFN0 + 4 * NG
U_SWA = U_KV + KV_SLOTS
U_FFN1 = U_SWA + 2 * KVH
ADA_UNITS = {0: 3, 1: 2, 3: 1, 4: 1, 5: 1, 6: 8, 7: 3, 8: 3, 9: 2}
RET_LOCAL = [j + sum(n for a, n in ADA_UNITS.items() if a < j) for j in range(RET_SLOTS)]
RET_FIRST = 3
D_FFN0 = 8 * RH
D_SWA = D_FFN0 + 2 * NG
D_FFN1 = D_SWA + 2 * KVH
N_FIRST = 2 * KT
FIRST_LOADS = (0, 4, 8, 12, 13, 14, 15)
E_LATER = (NVEC - 2) * KT
N_ENTRIES = N_SLOTS + E_LATER

C_ADAB = 0
C_NORM = C_ADAB + NVEC * KT
C_KVN = C_NORM + 8 * KT
C_CW = C_KVN + KT
C_CB = C_CW + 2 * 3 * 2 * FT
N_COLS = C_CB + 2 * 2 * FT

T_XI = 0
T_GINV = T_XI + RH * CH
T_ZETA = T_GINV + RH
T_GC = T_ZETA + RH
T_TRI = T_GC + RH
T_ID = T_TRI + CH
T_ONES = T_ID + P
N_TAB = T_ONES + P
BODY_UPS = (0, 1, 2, 3, 6, 7, 8, 9)
ML = 384


def trunk(nc, x_in, c_d, cols_d, first_d, stream_d, sinks_d, rel_d, rope_d, tab_d, hot_d, out):
    x_mid = [nc.dram_tensor(f"x_mid{i}", (S, D), F32).ap() for i in range(3)]
    k_dram = nc.dram_tensor("k_dram", (2 * P, S), F32).ap()
    bias_dram = nc.dram_tensor("bias_dram", (QH, P * ML), F32).ap()

    ctx = ExitStack()
    with ctx:
        offset = [nc.sbuf_base + (-nc.sbuf_base) % 32]

        def put(name, cols, dt=F32, at=None):
            where = offset[0] if at is None else at
            t = nc.alloc_sbuf_tensor_at(name, [P, cols], dt, offset=where)
            if at is None:
                offset[0] += 4 * cols + (-4 * cols) % 32
            return t, where

        h_t, h_at = put("H_hi", KT * S, F32R)
        H_hi = h_t.ap().rearrange("p (k s) -> p k s", k=KT)
        H_lo = put("H_lo", KT * S, F32R)[0].ap().rearrange("p (k s) -> p k s", k=KT)
        first = put("first", N_FIRST * 1024, at=h_at)[0].ap().rearrange("p (e c) -> p e c", e=N_FIRST)
        y_acc = put("y_acc", TT * D)[0].ap().rearrange("p (t d) -> p t d", t=TT)
        g_t, g_at = put("G_hi", 4 * S, F32R)
        G_hi = g_t.ap().rearrange("p (f s) -> p f s", f=4)
        G_lo = put("G_lo", 4 * S, F32R)[0].ap().rearrange("p (f s) -> p f s", f=4)
        qk = put("qk", 4 * S, at=g_at)[0].ap().rearrange("p (f s) -> p f s", f=4)
        turned = put("turned", 2 * 1024, at=g_at + 4 * 2 * S)[0].ap().rearrange("p (r c) -> p r c", r=2)
        raw = put("raw", 2 * 1024)[0].ap().rearrange("p (r c) -> p r c", r=2)
        W_hi = put("W_hi", 2 * 1024, F32R)[0].ap().rearrange("p (r c) -> p r c", r=2)
        W_lo = put("W_lo", 2 * 1024, F32R)[0].ap().rearrange("p (r c) -> p r c", r=2)
        scr = put("scratch", 4 * 1024)[0].ap().rearrange("p (f s) -> p f s", f=4)
        state = put("state", 2 * 1024)[0].ap().rearrange("p (r c) -> p r c", r=2)
        cols = put("cols", N_COLS)[0].ap()
        tab = put("tab", N_TAB)[0].ap()
        mods = put("mods", NVEC * KT)[0].ap()
        ada_sum = put("ada_sum", KT)[0].ap()
        amul = put("amul", KT)[0].ap()
        gvec = put("gvec", KT)[0].ap()
        ssq = put("ssq", 2 * TT)[0].ap()
        ms = put("ms", 2 * TT)[0].ap()
        rs = put("rs", 2 * TT)[0].ap()
        small = put("small", 64)[0].ap()
        nsink = put("nsink", QH)[0].ap()
        rel = put("rel", QH)[0].ap()
        shared_at = offset[0]
        rope = put("rope", 2 * S)[0].ap().rearrange("p (r s) -> p r s", r=2)
        gate_sb = put("gate", 2 * S, at=shared_at)[0].ap().rearrange("p (r s) -> p r s", r=2)
        x_more = put("x_more", 4 * D, at=shared_at + 4 * 2 * S)[0].ap().rearrange("p (r s) -> p r s", r=4)
        assert shared_at + 4 * (2 * S + 4 * D) <= nc.sbuf_usable_end
        c_row = put("c_row", D)[0].ap()
        k_sb = put("k_sb", 2 * DK)[0].ap().rearrange("p (r c) -> p r c", r=2)
        sm = put("sm", 2 * CH)[0].ap().rearrange("p (r c) -> p r c", r=2)
        on = put("on", 2 * DV)[0].ap().rearrange("p (r c) -> p r c", r=2)
        assert offset[0] <= nc.sbuf_usable_end, offset[0]
        offset[0] = shared_at
        qT = put("qT", 2 * S)[0].ap().rearrange("p (f s) -> p f s", f=2)
        kd = state[:, 0, :]
        vtok = put("vtok", NB * KVH * HD)[0].ap().rearrange("p (b c) -> p b c", b=NB)
        vg = put("vg", NB * HD)[0].ap().rearrange("p (b c) -> p b c", b=NB)
        bias = state[:, 1, :].rearrange("p (h c) -> p h c", h=4)
        stat = put("stat", 4 * 6 * 4)[0].ap().rearrange("p (r a h) -> p r a h", r=4, a=6)
        hot = put("hot", ML)[0].ap()
        brow = put("brow", ML)[0].ap()
        assert offset[0] <= nc.sbuf_usable_end, offset[0]

        tri = tab[:, T_TRI:T_TRI + CH]
        ident = tab[:, T_ID:T_ID + P]
        ones = tab[:, T_ONES:T_ONES + P]
        pows = small[:, 0:1]
        bn6 = small[:, 8:14]
        mv = small[:, 16:20].rearrange("p (r c) -> p r c", r=2)
        ve = small[:, 20:22]
        rv = small[:, 22:24]

        ps = ctx.enter_context(nc.psum_tensor("ps", [P, 8 * 512], F32))

        def bank(b, n=1):
            return ps[:, 512 * b:512 * (b + n)]

        def sem(name):
            return ctx.enter_context(nc.semaphore(name))

        landed = [sem("landed0"), sem("landed1")]
        first_in = [sem(f"first_in{i}") for i in range(len(FIRST_LOADS))]
        first_sum = sem("first_sum")
        used = sem("used")
        w_hi = sem("w_hi")
        slot_done = sem("slot_done")
        u_free = sem("u_free")
        d_ready, d_free = sem("d_ready"), sem("d_free")
        consts, tabs_in, apart = sem("consts"), sem("tabs_in"), sem("apart")
        rope_in = sem("rope_in")
        dve, rd_link, mx_link = sem("dve"), sem("rd_link"), sem("mx_link")
        a_bn, conv_mid = sem("a_bn"), sem("conv_mid")
        ada_out = sem("ada_out")
        y_zero = sem("y_zero")
        x_in_sem = [sem(f"x_in{t}") for t in range(TT)]
        x_out_sem = [sem(f"x_out{t}") for t in range(TT)]
        b_diag, b_row, b_gate = sem("b_diag"), sem("b_row"), sem("b_gate")
        b_sq, b_ms, b_rs, b_y, b_x, b_xn = (sem(n) for n in ("b_sq", "b_ms", "b_rs", "b_y", "b_x", "b_xn"))
        b_x_gp = sem("b_x_gp")
        t_ready, h_tmp, h_hi, h_lo = sem("t_ready"), sem("h_tmp"), sem("h_hi"), sem("h_lo")
        rot_add, k_rot = sem("rot_add"), sem("k_rot")
        a_kt, a_kv, a_s, a_m = (sem(n) for n in ("a_kt", "a_kv", "a_s", "a_m"))
        a_r, a_R, a_o, a_mv, a_ve, a_rs = (sem(n) for n in ("a_r", "a_R", "a_o", "a_mv", "a_ve", "a_rs"))
        a_on, a_ot, a_oe = (sem(n) for n in ("a_on", "a_ot", "a_oe"))
        g_sg, g_mul, g_hi, g_lo = (sem(n) for n in ("g_sg", "g_mul", "g_hi", "g_lo"))
        c_init = sem("c_init")
        kv_out, kv_vt, kv_vtok = sem("kv_out"), sem("kv_vt"), sem("kv_vtok")
        kd_in, bias_in, vg_in, ns_in = (sem(n) for n in ("kd_in", "bias_in", "vg_in", "ns_in"))
        r_set, r_in, r_mm, r_row, r_out = (sem(n) for n in ("r_set", "r_in", "r_mm", "r_row", "r_out"))
        s_qk, s_add, s_mx, s_ex = (sem(n) for n in ("s_qk", "s_add", "s_mx", "s_ex"))
        s_rd, s_p, s_pt, s_tp = (sem(n) for n in ("s_rd", "s_p", "s_pt", "s_tp"))
        s_pv, s_oh, s_ol = (sem(n) for n in ("s_pv", "s_oh", "s_ol"))

        stream = stream_d.rearrange("e p c -> p e c")
        first_units = first_d.rearrange("e p c -> p e c")
        bias_rows = bass.AP(bias_dram.tensor, P - 1, [[P * ML, QH], [ML - 1, P], [1, 2 * BLK]])

        def column(where, k):
            return cols[:, where + k:where + k + 1]

        def norm_at(layer, i):
            return C_NORM + (layer * 4 + i) * KT

        BOUNDARIES = [
            (None, None, x_in, None, norm_at(0, 0), M_SC_M0, M_SH_M0),
            (norm_at(0, 1), M_GT_M0, x_in, x_mid[0], norm_at(0, 2), M_SC_F0, M_SH_F0),
            (norm_at(0, 3), M_GT_F0, x_mid[0], x_mid[1], C_KVN, M_SC_KV, M_SH_KV),
            (norm_at(1, 1), M_GT_M1, x_mid[1], x_mid[2], norm_at(1, 2), M_SC_F1, M_SH_F1),
            (norm_at(1, 3), M_GT_F1, x_mid[2], out, None, None, None),
        ]
        SQ_BEFORE = [0, TT, 3 * TT, 5 * TT, 7 * TT]

        def squares_done(b, of_x, t):
            if b in (0, 4):
                return SQ_BEFORE[b] + t + 1
            if of_x:
                return SQ_BEFORE[b] + min(2 * t + 4, TT + t + 1)
            return SQ_BEFORE[b] + t + 1 + max(0, t - 2)

        def turn_counts(turn):
            return 2 * KT * turn

        def piece_landed(base, per, i, local):
            r = (base + local) % 2
            return r, 8 * per * i + 16 * ((base + local - r) // 2 + 1)

        def x_tile(t):
            return scr[:, t, :] if t < 4 else x_more[:, t - 4, :]

        AHEAD = 3
        GP_TILES = (0, 2, 4)

        def residual_done(b, t):
            ours = GP_TILES if t in GP_TILES else [i for i in range(TT) if i not in GP_TILES]
            return (b_x_gp if t in GP_TILES else b_x), len(ours) * (b - 1) + list(ours).index(t) + 1

        LAST_TILES = [(0, 0), (1, 0), (0, 1), (1, 1)] + [(t, half) for t in range(2, TT) for half in range(2)]
        TILES_WITH = [1 + LAST_TILES.index((t, 1)) for t in range(TT)]

        v_tok = scr.rearrange("p r c -> p (r c)").rearrange("p (c v) -> p c v", c=NC)
        head_out = v_tok.rearrange("p c (f s) -> p f c s", f=4)

        modded = state.rearrange("p r (q c) -> p (r q) c", q=2)

        block = ctx.enter_context(nc.Block())

        @block.sync
        def _(sp):
            for t in range(4):
                sp.dma_start(y_acc[:, t, :], x_in[P * t:P * (t + 1), :]).then_inc(x_in_sem[t], 16)
            for i, e in enumerate(FIRST_LOADS):
                part = slice(e, (FIRST_LOADS + (N_FIRST,))[i + 1])
                sp.dma_start(first[:, part, :], first_units[:, part, :]).then_inc(first_in[i], 16)
                if i == 1:
                    for r in range(2):
                        sp.dma_start(raw[:, r, :], stream[:, r, :]).then_inc(landed[r], 16)
            for t in range(4, TT):
                sp.dma_start(y_acc[:, t, :], x_in[P * t:P * (t + 1), :]).then_inc(x_in_sem[t], 16)
            sp.dma_start(rope, rope_d).then_inc(rope_in, 16)
            with sp.Fori(1, N_ENTRIES // 2) as i:
                for r in range(2):
                    sp.wait_ge(used, 2 * i + (r - 1))
                    sp.dma_start(raw[:, r:r + 1, :], stream[:, bass.ds(2 * i + r, 1), :]).then_inc(landed[r], 16)

        @block.tensor
        def _(pe):
            def weights(w, parts):
                return (W_hi[:, w, :].rearrange("p (k f) -> p k f", k=parts),
                        W_lo[:, w, :].rearrange("p (k f) -> p k f", k=parts))

            def up_part(j, half, k):
                wh, wl = weights(j % 2, KT)
                o = bank(2 * (j % 2) + half)
                tok = slice(HALF * half, HALF * (half + 1))
                nc.tensor.matmul(o, wh[:, k, :], H_hi[:, k, tok], start=(k == 0), stop=False)
                nc.tensor.matmul(o, wh[:, k, :], H_lo[:, k, tok], start=False, stop=False)
                return nc.tensor.matmul(o, wl[:, k, :], H_hi[:, k, tok], start=False, stop=(k == KT - 1))

            def up_ready(piece, u):
                pe.wait_ge(used, piece + 1)
                pe.wait_ge(u_free, u + 1)

            def up_slot(piece, u, j):
                up_ready(piece, u)
                for half in range(2):
                    for k in range(KT):
                        last = up_part(j, half, k)
                last.then_inc(slot_done, 1)

            def down_slot(piece, dslot, w, f0, acts_hi=G_hi, acts_lo=G_lo):
                pe.wait_ge(used, piece + 1)
                wh, wl = weights(w, 2)
                for t in range(TT):
                    pe.wait_ge(d_free, TT * dslot + (t + 1))
                    o = bank(4 + t % 2)
                    tok = slice(P * t, P * (t + 1))
                    for f in range(2):
                        nc.tensor.matmul(o, acts_hi[:, f0 + f, tok], wh[:, f, :], start=(f == 0), stop=False)
                        nc.tensor.matmul(o, acts_hi[:, f0 + f, tok], wl[:, f, :], start=False, stop=False)
                        last = nc.tensor.matmul(o, acts_lo[:, f0 + f, tok], wh[:, f, :], start=False, stop=(f == 1))
                    last.then_inc(d_ready if t < TT - 1 else slot_done, 1)

            def turn(number, i, xn_base):
                half, k = i // KT, i % KT
                if k == 0:
                    pe.wait_ge(b_xn, xn_base + 4 * (half + 1))
                if turn_counts(number) + i >= 2:
                    pe.wait_ge(h_tmp, turn_counts(number) + i - 1)
                for t in range(4):
                    last = nc.tensor.transpose(bank(6 + k % 2)[:, P * t:P * (t + 1)],
                                               y_acc[:, 4 * half + t, P * k:P * (k + 1)], ident)
                last.then_inc(t_ready, 1)

            def first_pair(piece, u, number, b):
                for i in range(AHEAD):
                    turn(number, i, TT * b)
                up_ready(piece, u)
                up_ready(piece + 1, u + 1)
                pe.wait_ge(b_sq, squares_done(b, True, 5))
                for half in range(2):
                    for k in range(KT):
                        i = KT * half + k
                        if i + AHEAD < 2 * KT:
                            turn(number, i + AHEAD, TT * b)
                        pe.wait_ge(h_lo, turn_counts(number) + i + 1)
                        last = up_part(0, half, k)
                        if half and k == KT - 1:
                            last.then_inc(slot_done, 1)
                        for k1 in {KT - 2: (), KT - 1: (KT - 2, KT - 1)}.get(k, (k,)):
                            last = up_part(1, half, k1)
                last.then_inc(slot_done, 1)

            def last_downs(b, piece, dslot, f0, u_before):
                pe.wait_ge(used, piece + 1)
                for idx, (t, half) in enumerate(LAST_TILES):
                    if idx == 2:
                        gate_row(b, u_before)
                        pe.wait_ge(used, piece + 2)
                    wh, wl = weights(half, 2)
                    pe.wait_ge(d_free, TT * dslot + (idx + 1))
                    o = bank(4 + idx % 2)
                    tok = slice(P * t, P * (t + 1))
                    for f in range(2):
                        nc.tensor.matmul(o, G_hi[:, f0 + f, tok], wh[:, f, :], start=(f == 0), stop=False)
                        nc.tensor.matmul(o, G_hi[:, f0 + f, tok], wl[:, f, :], start=False, stop=False)
                        last = nc.tensor.matmul(o, G_lo[:, f0 + f, tok], wh[:, f, :], start=False, stop=(f == 1))
                    last.then_inc(d_ready if t < TT - 1 else slot_done, 1)

            def gate_row(b, u_before):
                pe.wait_ge(b_diag, b)
                pe.wait_ge(u_free, u_before + 2)
                for half in range(2):
                    last = nc.tensor.matmul(bank(half), ones, gate_sb[:, 1, HALF * half:HALF * (half + 1)],
                                            start=True, stop=True)
                last.then_inc(b_row, 1)

            pe.wait_ge(tabs_in, 48)
            first_pair(0, 0, 0, 0)

            def retention_chunk(h, c, part):
                tok = slice(CH * c, CH * (c + 1))
                if part == "turn":
                    if c > 0:
                        pe.wait_ge(a_kv, 8 * h + c)
                    for i in range(2):
                        last = nc.tensor.transpose(bank(3)[:, P * i:P * (i + 1)], qk[:, 2 + i, tok], ident)
                    last.then_inc(a_kt, 1)
                if part == "scores":
                    if c > 0:
                        pe.wait_ge(a_m, 8 * h + c)
                    for i in range(2):
                        last = nc.tensor.matmul(bank(2)[:, 0:CH], qk[:, 2 + i, tok], qk[:, i, tok],
                                                start=(i == 0), stop=(i == 1))
                    last.then_inc(a_s, 1)
                if part == "state":
                    pe.wait_ge(a_kv, 8 * h + (c + 1))
                    if c > 0:
                        pe.wait_ge(a_R, 7 * h + c)
                    for i in range(2):
                        last = nc.tensor.matmul(bank(i), k_sb[:, c % 2, P * i:P * (i + 1)], v_tok[:, c, :],
                                                start=True, stop=True)
                    last.then_inc(a_r, 1)
                if part == "out":
                    if c == NC - 1:
                        pe.wait_ge(a_R, 7 * h + c)
                    pe.wait_ge(a_m, 8 * h + (c + 1))
                    o = bank(4 + c % 2)
                    last = nc.tensor.matmul(o, sm[:, c % 2, :], v_tok[:, c, :], start=True, stop=(c == 0))
                    if c > 0:
                        for i in range(2):
                            last = nc.tensor.matmul(o, qk[:, i, tok], state[:, c % 2, DV * i:DV * (i + 1)],
                                                    start=False, stop=(i == 1))
                    last.then_inc(a_o, 1)
                if part == "back":
                    pe.wait_ge(a_on, 8 * h + (c + 1))
                    if c > 0:
                        pe.wait_ge(a_oe, 8 * h + c)
                    for f in range(4):
                        last = nc.tensor.transpose(bank(7)[:, P * f:P * (f + 1)],
                                                   on[:, c % 2, P * f:P * (f + 1)], ident)
                    last.then_inc(a_ot, 1)

            def retention_head(h, last):
                u0 = RET_UPS * h + 2

                def piece(j):
                    return RET_ENTRIES * h + (RET_FIRST + (RET_LOCAL[j - 1] if j > 0 else -1))

                for j in range(2):
                    up_slot(piece(j), u0 + j, j)
                for j in range(2, 6):
                    down_slot(piece(j), 8 * h + (j - 2), j % 2, 2 * (j - 2), H_hi, H_lo)
                pe.wait_ge(u_free, u0 + 4)
                pe.wait_ge(rot_add, 4 * h + 4)
                pe.wait_ge(k_rot, h + 1)
                retention_chunk(h, 0, "turn")
                retention_chunk(h, 0, "scores")
                for c in range(NC):
                    if c < NC - 1:
                        retention_chunk(h, c + 1, "turn")
                        retention_chunk(h, c + 1, "scores")
                    if c == 0:
                        pe.wait_ge(d_free, 8 * TT * h + (4 * TT + 2))
                    if c < NC - 1:
                        retention_chunk(h, c, "state")
                    retention_chunk(h, c, "out")
                    if c > 0:
                        retention_chunk(h, c - 1, "back")
                for j in range(6, 10):
                    up_slot(piece(j), u0 + (j - 4), j)
                    if j == 6:
                        retention_chunk(h, NC - 1, "back")
                if last:
                    pe.wait_ge(g_lo, 4 * h + 2)
                    for j in range(10, 12):
                        down_slot(piece(j), 8 * h + (j - 6), j % 2, 0)
                    pe.wait_ge(g_lo, 4 * h + 4)
                    last_downs(1, piece(12), 8 * h + 6, 2, U_FFN0)
                else:
                    for j in range(10, 14):
                        pe.wait_ge(g_lo, 4 * h + (2 if j < 12 else 4))
                        down_slot(piece(j), 8 * h + (j - 6), j % 2, 0 if j < 12 else 2)
                    for j in range(14, 16):
                        up_slot(piece(j), u0 + (j - 8), j)

            with pe.Fori(0, RH - 1) as h:
                retention_head(h, False)
            retention_head(RH - 1, True)

            def ffn(n0, u0, d0, g0, number, b):
                def up_group(n, u, start=0):
                    for j in range(start, 4):
                        up_slot(n + (E_LATER + j), u + j, j)

                def down_group(n, dslot, group, parity):
                    pe.wait_ge(g_lo, g0 + 2 * group + 2)
                    for j in range(2):
                        down_slot(n + (E_LATER + j), dslot + j, j % 2, 2 * parity)

                first_pair(n0 + E_LATER, u0, number, b)
                up_group(n0, u0, start=2)
                with pe.Fori(0, NG // 2) as i:
                    n, u, d = n0 + 4 + 12 * i, u0 + 4 + 8 * i, d0 + 4 * i
                    up_group(n, u)
                    down_group(n + 4, d, 2 * i, 0)
                    up_group(n + 6, u + 4)
                    down_group(n + 10, d + 2, 2 * i + 1, 1)
                pe.wait_ge(g_lo, g0 + FT)
                last_downs(b + 1, n0 + (FFN_SLOTS - 2) + E_LATER, d0 + 2 * NG - 2, 0, u0 + 4 * NG)

            ffn(N_FFN0, U_FFN0, D_FFN0, 4 * RH, 1, 1)

            piece_kv = N_KV + E_LATER
            first_pair(piece_kv, U_KV, 2, 2)
            pe.wait_ge(r_in, 32)
            pe.wait_ge(b_sq, SQ_BEFORE[3])
            nc.tensor.matmul(bank(4)[0:QH, 0:ML], rel[0:33, 0:QH], hot[0:33, :], start=True,
                             stop=True).then_inc(r_mm, 1)
            for j in (2, 3):
                up_ready(piece_kv + j, U_KV + j)
                for k in range(KT):
                    up_part(j, 0, k)
            for j in (2, 3):
                for k in range(KT):
                    if k % 2 == 0:
                        turn(3, 4 * (j - 2) + k // 2, 2 * TT)
                    last = up_part(j, 1, k)
                last.then_inc(slot_done, 1)
            for j in range(2):
                up_ready(N_SWA + E_LATER + j, U_SWA + j)
                for k in range(KT):
                    if k % 2 == 0:
                        turn(3, KT + 4 * j + k // 2, 2 * TT)
                    pe.wait_ge(h_lo, turn_counts(3) + k + 1)
                    up_part(j, 0, k)
            pe.wait_ge(r_row, 1)
            for b in range(NB):
                if b >= 2:
                    pe.wait_ge(kv_vtok, b - 1)
                for f in range(2):
                    last = nc.tensor.transpose(bank(4 + b % 2)[:, P * f:P * (f + 1)],
                                               scr[:, 2 + f, BLK * b:BLK * (b + 1)], ident)
                last.then_inc(kv_vt, 1)
            for j in range(2):
                for k in range(KT):
                    pe.wait_ge(h_lo, turn_counts(3) + KT + k + 1)
                    last = up_part(j, 1, k)
                last.then_inc(slot_done, 1)
            pe.wait_ge(kv_vtok, NB)

            def scores(g, s):
                if s >= 2:
                    pe.wait_ge(s_add, NB * g + (s - 1))
                for half in range(2):
                    for i in range(2):
                        q = qT[HD * half:HD * (half + 1), i, BLK * s:BLK * (s + 1)]
                        lo = BLK * (s - 1) if s > 0 else 0
                        wide = 2 * BLK if s > 0 else BLK
                        o = bank(2 * (s % 2) + half)[:, 256 * i + 256 - wide:256 * i + 256]
                        last = nc.tensor.matmul(o, q, kd[HD * half:HD * (half + 1), lo:lo + wide],
                                                start=True, stop=True)
                last.then_inc(s_qk, 1)

            def probs_turned(g, s):
                pe.wait_ge(s_p, NB * g + (s + 1))
                if s >= 1:
                    pe.wait_ge(s_tp, NB * g + s)
                for part in ((0, 1) if s > 0 else (1,)):
                    for hd in range(4):
                        last = nc.tensor.transpose(bank(6 + part)[:, P * hd:P * (hd + 1)],
                                                   scr[:, s % 4, 256 * hd + P * part:256 * hd + P * part + P],
                                                   ident)
                last.then_inc(s_pt, 1)

            def weighted(g, s):
                pe.wait_ge(s_tp, NB * g + (s + 1))
                if s == 0:
                    pe.wait_ge(vg_in, g + 1)
                    pe.wait_ge(d_free, 2 * TT * g + (TT * D_SWA + 2))
                if s >= 2:
                    pe.wait_ge(s_ol, NB * g + (s - 1))
                parts = (0, 1) if s > 0 else (1,)
                for half in range(2):
                    o = bank(4 + s % 2)[HD * half:HD * (half + 1), 0:256]
                    for part in parts:
                        last = nc.tensor.matmul(o, vg[:, s - 1 + part, :],
                                                turned[:, s % 2, 512 * part + 256 * half:512 * part + 256 * half + 256],
                                                start=(part == parts[0]), stop=(part == parts[-1]))
                last.then_inc(s_pv, 1)

            def first_scores(g):
                pe.wait_ge(u_free, 2 * g + (U_SWA + 4))
                pe.wait_ge(kd_in, 32 * g + 32)
                scores(g, 0)
                scores(g, 1)

            def attention(g, last):
                n0, u0 = SWA_SLOTS * g + (N_SWA + 2), 2 * g + (U_SWA + 2)
                piece = n0 + E_LATER
                for s in range(2, NB + 4):
                    if s < NB:
                        scores(g, s)
                    elif not last:
                        j, half = (s - NB) // 2, (s - NB) % 2
                        if half == 0:
                            up_ready(piece + j, u0 + j)
                            pe.wait_ge(s_add, NB * g + (NB - 1 + j))
                        if s == NB + 3:
                            weighted(g, NB - 1)
                        for k in range(KT):
                            done = up_part(j, half, k)
                        if half:
                            done.then_inc(slot_done, 1)
                    if 3 <= s < NB + 3:
                        probs_turned(g, s - 3)
                    if s >= 4 and (last or s < NB + 3):
                        weighted(g, s - 4)
                pe.wait_ge(s_ol, NB * g + NB)
                if last:
                    last_downs(3, piece, 2 * g + D_SWA, 0, U_FFN1)
                else:
                    down_slot(piece + 2, 2 * g + D_SWA, 0, 0)
                    first_scores(g + 1)
                    down_slot(piece + 3, 2 * g + (D_SWA + 1), 1, 0)

            first_scores(0)
            with pe.Fori(0, KVH - 1) as g:
                attention(g, False)
            attention(KVH - 1, True)

            ffn(N_FFN1, U_FFN1, D_FFN1, 4 * RH + FT, 4, 3)

        @block.scalar
        def _(act):
            def split(n, piece, w):
                r, value = piece
                act.wait_ge(landed[r], value)
                act.wait_ge(slot_done, n + 1)
                nc.scalar.activation(W_hi[:, w, :], raw[:, r, :], ACT.Copy).then_inc(w_hi, 1)

            def sum_squares(b, of_x, t):
                count = squares_done(b, of_x, t)
                if count > 1:
                    act.wait_ge(b_sq, count - 1)
                src, col = (x_tile(t) if b > 0 else y_acc[:, t, :], TT + t) if of_x else (y_acc[:, t, :], t)
                nc.scalar.activation(bank(4 if of_x and t >= 6 else 2, 2), src, ACT.Square,
                                     accum_out=ssq[:, col:col + 1]).then_inc(b_sq, 1)

            def load_x(b, t):
                act.dma_start(x_tile(t), BOUNDARIES[b][2][P * t:P * (t + 1), :]).then_inc(x_in_sem[t], 16)

            def normalise(b, t):
                act.wait_ge(b_rs, squares_done(b, True, t))
                nc.scalar.activation(y_acc[:, t, :], x_tile(t) if b > 0 else y_acc[:, t, :], ACT.Copy,
                                     scale=rs[:, TT + t:TT + t + 1]).then_inc(b_xn, 1)

            def turn_hi(number, units):
                for i in units:
                    half, k = i // KT, i % KT
                    act.wait_ge(h_tmp, turn_counts(number) + i + 1)
                    nc.scalar.activation(H_hi[:, k, HALF * half:HALF * (half + 1)], modded[:, i % 4, :],
                                         ACT.Copy).then_inc(h_hi, 1)

            def boundary(b, number, n, piece, d_slots, g_count):
                _, _, _, x_new, norm_g, _, _ = BOUNDARIES[b]

                def next_split(m):
                    split(n + m, piece_landed(piece + m, 0, 0, 0), m % 2)

                if b != 3:
                    next_split(1)
                act.wait_ge(g_lo, g_count)
                for t in range(TT):
                    load_x(b, t)
                act.wait_ge(b_row, b)
                nc.scalar.activation(gate_sb[:, 0, :], bank(0, 2), ACT.Copy).then_inc(b_gate, 1)
                for i in range(TT + 2):
                    if i < TT:
                        act.wait_ge(d_free, TT * (d_slots - 2) + 2 + TILES_WITH[i])
                        sum_squares(b, False, i)
                    if i == TT - 1 and norm_g is not None:
                        next_split(2)
                        next_split(3)
                    if i >= 2:
                        t = i - 2
                        act.wait_ge(*residual_done(b, t))
                        act.dma_start(x_new[P * t:P * (t + 1), :], x_tile(t)).then_inc(x_out_sem[t], 16)
                        if norm_g is not None:
                            sum_squares(b, True, t)
                            if t > 0:
                                normalise(b, t - 1)
                    if i == TT and norm_g is not None:
                        turn_hi(number, range(AHEAD))
                if norm_g is not None:
                    normalise(b, TT - 1)
                    turn_hi(number, range(AHEAD, 2 * KT))
                for t in range(TT):
                    act.wait_ge(x_out_sem[t], 16 * b)

            act.dma_start(cols, cols_d).then_inc(tabs_in, 16)
            act.dma_start(tab, tab_d).then_inc(tabs_in, 16)
            act.dma_start(c_row, c_d.to_broadcast([P, D])).then_inc(tabs_in, 16)
            act.wait_ge(tabs_in, 48)
            nc.scalar.activation(c_row, c_row, ACT.Silu).then_inc(consts, 1)
            for t in range(TT):
                if t == 4:
                    for n in range(2):
                        split(n, piece_landed(n, 0, 0, 0), n)
                act.wait_ge(x_in_sem[t], 16)
                sum_squares(0, True, t)
                if t >= 4:
                    turn_hi(0, range(2 * t - 8, 2 * t - 6))
                normalise(0, t)
            turn_hi(0, range(KT, 2 * KT))
            split(2, piece_landed(2, 0, 0, 0), 0)

            def retention_head(h, last):
                n0 = RET_SLOTS * h + 2
                for j in range(12 if last else RET_SLOTS):
                    def next_split():
                        split(n0 + (j + 1), piece_landed(RET_FIRST, RET_ENTRIES, h, RET_LOCAL[j]), (j + 1) % 2)

                    if j != 6:
                        next_split()
                    else:
                        for c in range(NC + 2):
                            if c < NC:
                                act.wait_ge(a_kt, 8 * h + c + 1)
                                act.sem_inc(apart, 1)
                                nc.scalar.activation(k_sb[:, c % 2, :], bank(3)[:, 0:DK], ACT.Copy,
                                                     scale=tab[:, bass.ds(h + T_ZETA, 1)]).then_inc(a_kv, 1)
                            if c == 0:
                                next_split()
                            if c > 1:
                                act.wait_ge(a_ot, 8 * h + (c - 1))
                                nc.scalar.activation(v_tok[:, c - 2, :], bank(7), ACT.Copy).then_inc(a_oe, 1)
                    if 7 <= j <= 10:
                        f = j - 7
                        act.wait_ge(slot_done, n0 + (j + 2))
                        if f >= 2:
                            act.wait_ge(g_mul, 4 * h + f - 1)
                        nc.scalar.activation(state[:, f % 2, :], bank(2 * ((j - 1) % 2), 2),
                                             ACT.Silu).then_inc(u_free, 1)
                        act.wait_ge(g_mul, 4 * h + f + 1)
                        nc.scalar.activation(G_hi[:, f, :].rearrange("p (c s) -> p c s", c=NC), head_out[:, f, :, :],
                                             ACT.Copy).then_inc(g_hi, 1)

            with act.Fori(0, RH - 1) as h:
                retention_head(h, False)
            retention_head(RH - 1, True)
            boundary(1, 1, N_FFN0 - 2, N_FFN0 - 2 + E_LATER, D_FFN0, 4 * RH)

            def ffn(layer, n0, u0, g0):
                def take(val, f, u, done, fp, buf, scratch_free=None):
                    act.wait_ge(slot_done, done)
                    if scratch_free is not None:
                        act.wait_ge(g_lo, scratch_free)
                    wcol = C_CW + (layer * 3 + 2) * 2 * FT + val * FT
                    bcol = C_CB + layer * 2 * FT + val * FT
                    act.sem_inc(apart, 1)
                    nc.scalar.activation(scr[:, 2 * fp + val, :], bank(2 * val, 2), ACT.Identity,
                                         bias=cols[:, bass.ds(f + bcol, 1)],
                                         scale=cols[:, bass.ds(f + wcol, 1)]).then_inc(c_init, 1)
                    if val:
                        act.wait_ge(u_free, u + 2)
                        nc.scalar.activation(scr[:, 2 * fp, :], scr[:, 2 * fp, :], ACT.Silu).then_inc(g_sg, 1)
                        act.wait_ge(g_mul, f + (g0 + 1))
                        nc.scalar.activation(G_hi[:, buf, :], scr[:, 2 * fp + 1, :], ACT.Copy).then_inc(g_hi, 1)

                for j in range(1, 4):
                    split(n0 + j + 1, piece_landed(n0 + E_LATER + 1, 0, 0, j), (j + 1) % 2)
                    take((j - 1) % 2, (j - 1) // 2, u0 + j - 1, n0 + j + 2, (j - 1) // 2, (j - 1) // 2)
                take(1, 1, u0 + 3, n0 + 6, 1, 1)
                with act.Fori(0, NG // 2) as i:
                    n, u = 12 * i + (n0 + 4), 8 * i + (u0 + 4)
                    for j in range(12):
                        split(n + (j + 1), piece_landed(n0 + 4 + E_LATER + 1, 12, i, j), (j + 1) % 2)
                        if j - 1 in BODY_UPS:
                            q = BODY_UPS.index(j - 1)
                            f = 4 * i + (2 + q // 2)
                            take(q % 2, f, u + q, n + (j + 2), (q // 2) % 2, (2 + q // 2) % 4,
                                 f + (g0 - 1) if q % 2 == 0 else None)

            ffn(0, N_FFN0, U_FFN0, 4 * RH)
            boundary(2, 2, N_KV - 2, N_KV - 2 + E_LATER, D_SWA, 4 * RH + FT)
            act.wait_ge(r_set, 1)
            act.dma_start(rel[0:32, :], rel_d).then_inc(r_in, 16)
            act.dma_start(hot[0:33, :], hot_d).then_inc(r_in, 16)

            def take_kv(j):
                act.wait_ge(slot_done, N_KV + j + 3)
                nc.scalar.activation(scr[:, j, :], bank(2 * (j % 2), 2), ACT.Copy).then_inc(u_free, 1)

            def split_later(n):
                split(n, piece_landed(n + E_LATER, 0, 0, 0), n % 2)

            for j in range(2):
                split_later(N_KV + 2 + j)
                take_kv(j)
            act.wait_ge(u_free, U_KV + 4)
            for f in range(2):
                act.dma_start(k_dram[P * f:P * (f + 1), :], scr[:, f, :]).then_inc(kv_out, 16)
            act.wait_ge(r_mm, 1)
            nc.scalar.activation(brow[0:QH, :], bank(4)[0:QH, 0:ML], ACT.Copy).then_inc(r_row, 1)
            act.wait_ge(r_row, 1)
            act.dma_start(bias_dram.rearrange("h (r m) -> h r m", m=ML),
                          brow[0:QH, :].unsqueeze(1).to_broadcast([QH, P, ML])).then_inc(r_out, 16)
            turn_hi(3, range(KT))
            for j in range(2):
                split_later(N_SWA + j)
                take_kv(2 + j)
            turn_hi(3, range(KT, 2 * KT))
            for b in range(NB):
                act.wait_ge(kv_vt, b + 1)
                nc.scalar.activation(vtok[:, b, :], bank(4 + b % 2)[:, 0:2 * P], ACT.Copy).then_inc(kv_vtok, 1)
            act.wait_ge(h_lo, turn_counts(4))
            act.wait_ge(kv_out, 32)
            act.wait_ge(r_out, 16)

            def load_keys_and_bias(g):
                for half in range(2):
                    act.dma_start(kd[HD * half:HD * (half + 1), :], k_dram[bass.ds(HD * g, HD), :]).then_inc(kd_in, 16)
                act.dma_start(bias, bias_rows[bass.ds(4 * g, 4), :, :].rearrange("h p c -> p h c")).then_inc(bias_in, 16)

            def take_q(n, i):
                act.wait_ge(slot_done, n + 3)
                nc.scalar.activation(qT[:, i, :], bank(2 * i, 2), ACT.Copy, scale=HD ** -0.5).then_inc(u_free, 1)

            def exponentials(g, s):
                act.wait_ge(s_mx, NB * g + (s + 1))
                w0 = 0 if s > 0 else BLK
                for hd in range(4):
                    e = scr[:, s % 4, 256 * hd + w0:256 * hd + 256]
                    nc.scalar.activation(e, e, ACT.Exp, bias=stat[:, s % 4, 1, hd:hd + 1],
                                         accum_out=stat[:, s % 4, 2, hd:hd + 1])
                nc.scalar.activation(stat[:, s % 4, 3, :], stat[:, s % 4, 4, :], ACT.Exp).then_inc(s_ex, 1)

            load_keys_and_bias(0)
            split_later(N_SWA + 2)
            take_q(N_SWA, 0)
            take_q(N_SWA + 1, 1)
            for s in range(2):
                exponentials(0, s)

            def attention(g, last):
                n0 = SWA_SLOTS * g + (N_SWA + 2)

                def split_slot(m):
                    split(n0 + m, piece_landed(N_SWA + 2 + E_LATER, SWA_SLOTS, g, m), m % 2)

                for s in range(2, NB + 5):
                    if s >= 5:
                        b = s - 5
                        act.wait_ge(s_pv, NB * g + (b + 1))
                        nc.scalar.activation(G_hi[:, 0:2, BLK * b:BLK * (b + 1)],
                                             bank(4 + b % 2)[:, 0:256].rearrange("p (f s) -> p f s", f=2),
                                             ACT.Copy).then_inc(s_oh, 1)
                    if 3 <= s < NB + 3:
                        first = 512 if s == 3 else 0
                        act.wait_ge(s_pt, NB * g + (s - 2))
                        nc.scalar.activation(turned[:, (s - 3) % 2, first:], bank(6, 2)[:, first:],
                                             ACT.Copy).then_inc(s_tp, 1)
                    if s < NB:
                        exponentials(g, s)
                    if s == 4:
                        split_slot(1)
                if not last:
                    load_keys_and_bias(g + 1)
                    for j in range(2):
                        split_slot(2 + j)
                        take_q(n0 + j, j)
                    for s in range(2):
                        exponentials(g + 1, s)
                    split_slot(4)

            with act.Fori(0, KVH - 1) as g:
                attention(g, False)
            attention(KVH - 1, True)

            act.wait_ge(s_ol, NB * KVH)
            boundary(3, 4, N_FFN1 - 2, N_FFN1 - 2 + E_LATER, D_FFN1, 4 * RH + FT)
            ffn(1, N_FFN1, U_FFN1, 4 * RH + FT)
            boundary(4, None, N_SLOTS - 2, N_SLOTS - 2 + E_LATER, D_FFN1 + 2 * NG, 4 * RH + 2 * FT)

        @block.vector
        def _(v):
            links = [0]

            def link(ins):
                links[0] += 1
                ins.then_inc(dve, 1)
                v.wait_ge(dve, links[0])

            def split(n, r, w):
                v.wait_ge(w_hi, n + 1)
                nc.vector.tensor_tensor(W_lo[:, w, :], raw[:, r, :], W_hi[:, w, :].bitcast(F32),
                                        ALU.subtract).then_inc(used, 1)

            def weighted_sum(weights, out):
                return nc.vector.scalar_tensor_tensor(weights, weights, 1.0, c_row, ALU.mult, ALU.mult, accum_out=out)

            def ada_unit(k, piece):
                r, value = piece
                v.wait_ge(landed[r], value)
                weighted_sum(raw[:, r, :], ada_sum[:, k:k + 1]).then_inc(used, 1)

            def ada_column(vec, piece):
                v.wait_ge(used, piece + 1)
                nc.vector.tensor_tensor(mods[:, bass.ds(KT * vec, KT)], ada_sum,
                                        cols[:, bass.ds(KT * vec + C_ADAB, KT)], ALU.add).then_inc(ada_out, 1)
                v.wait_ge(ada_out, vec - 1)

            def gain(dst, scale, g_col):
                return nc.vector.scalar_tensor_tensor(dst, mods[:, KT * scale:KT * (scale + 1)], 1.0,
                                                      cols[:, g_col:g_col + KT], ALU.add, ALU.mult)

            def turn_tmp(number, shift, units):
                for i in units:
                    k = i % KT
                    v.wait_ge(t_ready, turn_counts(number) + i + 1)
                    if i >= 4 or number > 0:
                        v.wait_ge(h_lo, turn_counts(number) + i - 3)
                    nc.vector.tensor_scalar(modded[:, i % 4, :], bank(6 + k % 2),
                                            amul[:, k:k + 1], mods[:, KT * shift + k:KT * shift + k + 1],
                                            ALU.mult, ALU.add).then_inc(h_tmp, 1)

            def boundary(b, number, n, dslot):
                norm_y, gate, _, _, norm_g, scale, shift = BOUNDARIES[b]
                v.wait_ge(ada_out, NVEC - 2)
                if norm_g is not None:
                    link(gain(amul, scale, norm_g))
                link(gain(gvec, gate, norm_y))
                nc.vector.tensor_tensor(gate_sb[:, 1, :].rearrange("p (k f) -> p k f", k=KT),
                                        ident.unsqueeze(1).to_broadcast([P, KT, P]),
                                        gvec.unsqueeze(2).to_broadcast([P, KT, P]), ALU.mult).then_inc(b_diag, 1)
                if b != 3:
                    split(n + 1, (n + 1) % 2, 1)

                def add_to_residual(t):
                    v.wait_ge(b_rs, squares_done(b, False, t))
                    nc.vector.scalar_tensor_tensor(y_acc[:, t, :], y_acc[:, t, :], rs[:, t:t + 1],
                                                   gate_sb[:, 0, :], ALU.mult, ALU.mult).then_inc(b_y, 1)
                    if t not in GP_TILES:
                        v.wait_ge(b_y, TT * (b - 1) + t + 1)
                        v.wait_ge(x_in_sem[t], 16 * (b + 1))
                        nc.vector.tensor_tensor(x_tile(t), x_tile(t), y_acc[:, t, :], ALU.add).then_inc(b_x, 1)

                done = 0
                for i in range(TT):
                    for idx in range(done, TILES_WITH[i]):
                        t, half = LAST_TILES[idx]
                        if t < TT - 1:
                            v.wait_ge(d_ready, (TT - 1) * dslot + idx + 1)
                        else:
                            v.wait_ge(slot_done, n + half + 3)
                        y = y_acc[:, t, HALF * half:HALF * (half + 1)]
                        nc.vector.tensor_tensor(y, bank(4 + idx % 2), y, ALU.add).then_inc(d_free, 1)
                    done = TILES_WITH[i]
                    if i == 0:
                        continue
                    if i == 1:
                        v.wait_ge(b_gate, b)
                    add_to_residual(i - 1)
                if norm_g is not None:
                    for m in (2, 3):
                        split(n + m, (n + m) % 2, m % 2)
                    turn_tmp(number, shift, range(AHEAD))
                add_to_residual(TT - 1)
                if norm_g is not None:
                    turn_tmp(number, shift, range(AHEAD, 2 * KT))

            def add_tile(t, half, ready, value):
                v.wait_ge(ready, value)
                y = y_acc[:, t, HALF * half:HALF * (half + 1)]
                nc.vector.tensor_tensor(y, bank(4 + t % 2), y, ALU.add).then_inc(d_free, 1)

            def down_step(n, dslot, half, others, after=range(0, TT, 2), add_tile=add_tile):
                others = list(others)
                for t in range(TT):
                    if t < TT - 1:
                        add_tile(t, half, d_ready, (TT - 1) * dslot + (t + 1))
                    else:
                        add_tile(t, half, slot_done, n + 3)
                    if others and t in after:
                        others.pop(0)()

            v.wait_ge(consts, 1)
            for e in range(N_FIRST):
                if e in FIRST_LOADS:
                    v.wait_ge(first_in[FIRST_LOADS.index(e)], 16)
                if e == KT:
                    for n in range(2):
                        split(n, n, n)
                weighted_sum(first[:, e, :], mods[:, e:e + 1]).then_inc(first_sum, 1)
            v.wait_ge(first_sum, N_FIRST)
            link(nc.vector.tensor_tensor(mods[:, 0:N_FIRST], mods[:, 0:N_FIRST], cols[:, C_ADAB:C_ADAB + N_FIRST],
                                         ALU.add))
            link(gain(amul, M_SC_M0, norm_at(0, 0)))
            turn_tmp(0, M_SH_M0, range(2 * KT))

            def rotate(n, i, part, which="both"):
                v.wait_ge(slot_done, n + 3)
                x = bank(2 * part, 2)
                sin_to, cos_to = scr[:, 2 * i + part, :], qk[:, 2 * i + part, :]
                if which != "sin":
                    nc.vector.tensor_tensor(cos_to, x, rope[:, 0, :], ALU.mult)
                if which != "cos":
                    nc.vector.tensor_tensor(sin_to, x, rope[:, 1, :], ALU.mult).then_inc(u_free, 1)

            split(2, 0, 0)
            v.wait_ge(rope_in, 16)
            rotate(0, 0, 0)

            def retention_head(h, last):
                n0, vec0 = RET_SLOTS * h + 2, 3 * h + 2

                def next_unit(j, i, k):
                    ada_unit(k, piece_landed(RET_FIRST, RET_ENTRIES, h, RET_LOCAL[j] + 1 + i))

                def column_done(vec, j):
                    ada_column(vec, RET_ENTRIES * h + (RET_FIRST + RET_LOCAL[j] + ADA_UNITS[j]))

                for j in range(12 if last else RET_SLOTS):
                    def next_split():
                        split(n0 + (j + 1), (RET_FIRST + RET_LOCAL[j]) % 2, (j + 1) % 2)

                    def add_value(t, half, ready, value):
                        v.wait_ge(ready, value)
                        if j == 2 and t == 0:
                            v.wait_ge(rot_add, 4 * h + 3)
                        if j == 2 and t == 4:
                            v.wait_ge(k_rot, h + 1)
                        if j == 2 and t == 6:
                            v.wait_ge(rot_add, 4 * h + 4)
                        tile = v_tok[:, t, :]
                        if j == 2:
                            nc.vector.tensor_copy(tile, bank(4 + t % 2)).then_inc(d_free, 1)
                        else:
                            nc.vector.tensor_tensor(tile, bank(4 + t % 2), tile, ALU.add).then_inc(d_free, 1)

                    def key_sum():
                        v.wait_ge(u_free, RET_UPS * h + 6)
                        nc.vector.tensor_tensor(qk[:, 3, :], qk[:, 3, :], scr[:, 2, :], ALU.add).then_inc(k_rot, 1)

                    if j == 2:
                        down_step(n0 + 2, 8 * h, 0, [lambda: rotate(n0 + 1, 1, 1, "cos"),
                                                     lambda: rotate(n0 + 1, 1, 1, "sin"), key_sum, next_split],
                                  after=(0, 1, 3, 5), add_tile=add_value)
                    elif 3 <= j < 6:
                        down_step(n0 + j, 8 * h + (j - 2), 0, [next_split], add_tile=add_value)
                    elif 10 <= j < 14:
                        down_step(n0 + j, 8 * h + (j - 6), j % 2, [next_split])
                    elif j != 6:
                        next_split()
                    if j <= 1:
                        rotate(n0 + (j - 1), (j + 1) // 2, (j + 1) % 2)
                    if j == 15:
                        rotate(n0 + 14, 0, 0)
                    if j == 7:
                        column_done(vec0 + 1, 6)
                    if j == 10:
                        column_done(vec0 + 2, 9)
                    if j in ADA_UNITS and j != 6:
                        for i in range(ADA_UNITS[j]):
                            next_unit(j, i, (sum(n for a, n in ADA_UNITS.items() if a < j) + i) % KT)
                    if j == 6:
                        def masked(c):
                            v.wait_ge(a_s, 8 * h + (c + 1))
                            nc.vector.scalar_tensor_tensor(sm[:, c % 2, :], bank(2)[:, 0:CH],
                                                           tab[:, bass.ds(h + T_GINV, 1)], tri,
                                                           ALU.mult, ALU.mult).then_inc(a_m, 1)

                        masked(0)
                        next_split()
                        column_done(vec0, 5)
                        for c in range(NC):
                            if c < NC - 1:
                                masked(c + 1)
                                v.wait_ge(a_r, 7 * h + (c + 1))
                                new = state[:, (c + 1) % 2, :]
                                if c == 0:
                                    nc.vector.tensor_copy(new, bank(0, 2)).then_inc(a_R, 1)
                                else:
                                    v.wait_ge(a_R, 7 * h + c)
                                    nc.vector.scalar_tensor_tensor(new, state[:, c % 2, :],
                                                                   tab[:, bass.ds(h + T_GC, 1)], bank(0, 2),
                                                                   ALU.mult, ALU.add).then_inc(a_R, 1)
                            v.wait_ge(a_o, 8 * h + (c + 1))
                            nc.vector.bn_stats(bn6, bank(4 + c % 2)).then_inc(a_bn, 1)
                            v.wait_ge(a_bn, 8 * h + (c + 1))
                            v.sem_inc(apart, 1)
                            nc.vector.bn_aggr(mv[:, c % 2, :], bn6).then_inc(a_mv, 1)
                            v.wait_ge(a_rs, 8 * h + (c + 1))
                            nc.vector.tensor_scalar(on[:, c % 2, :], bank(4 + c % 2), mv[:, c % 2, 0:1],
                                                    rv[:, c % 2:c % 2 + 1], ALU.subtract, ALU.mult).then_inc(a_on, 1)
                            next_unit(6, c, c)

            with v.Fori(0, RH - 1) as h:
                retention_head(h, False)
            retention_head(RH - 1, True)
            boundary(1, 1, N_FFN0 - 2, D_FFN0 - 2)

            def ffn(layer, n0, u0, d0, zero):
                c0 = 2 * FT * layer

                def conv(val, f, q, fp):
                    dst, src = scr[:, 2 * fp + val, :], bank(2 * val, 2)
                    col = C_CW + layer * 3 * 2 * FT + val * FT

                    def one_back():
                        v.wait_ge(c_init, q + (c0 + 1))
                        nc.vector.scalar_tensor_tensor(dst[:, 1:], src[:, :S - 1],
                                                       cols[:, bass.ds(f + (col + 2 * FT), 1)], dst[:, 1:],
                                                       ALU.mult, ALU.add).then_inc(conv_mid, 1)

                    def two_back():
                        v.wait_ge(conv_mid, q + (c0 + 1))
                        nc.vector.scalar_tensor_tensor(dst[:, 2:], src[:, :S - 2],
                                                       cols[:, bass.ds(f + col, 1)], dst[:, 2:],
                                                       ALU.mult, ALU.add).then_inc(u_free, 1)

                    return [one_back, two_back]

                def run(steps):
                    for step in steps:
                        step()

                for j in range(1, 4):
                    split(n0 + j + 1, (j + 1) % 2, (j + 1) % 2)
                    run(conv((j - 1) % 2, (j - 1) // 2, j - 1, (j - 1) // 2))
                run(conv(1, 1, 3, 1))
                v.wait_ge(y_zero, zero)
                with v.Fori(0, NG // 2) as i:
                    n = 12 * i + (n0 + 4)
                    for j in range(12):
                        work = [lambda: split(n + (j + 1), (j + 1) % 2, (j + 1) % 2)]
                        if j - 1 in BODY_UPS:
                            q = BODY_UPS.index(j - 1)
                            work += conv(q % 2, 4 * i + (2 + q // 2), 8 * i + (4 + q), (q // 2) % 2)
                        if j in BODY_UPS:
                            run(work)
                        else:
                            dslot = 4 * i + (d0 + (j - 4 if j < 6 else j - 8))
                            down_step(n + j, dslot, j % 2, work)

            ffn(0, N_FFN0, U_FFN0, D_FFN0, 2)
            boundary(2, 2, N_KV - 2, D_SWA - 2)

            for j in range(2):
                split(N_KV + 2 + j, j, j)
            link(gain(amul, M_SC_M1, norm_at(1, 0)))
            turn_tmp(3, M_SH_M1, range(KT))
            for j in range(2):
                split(N_SWA + j, j, j)
            turn_tmp(3, M_SH_M1, range(KT, 2 * KT))
            v.wait_ge(ns_in, 16)
            link(nc.vector.tensor_scalar(nsink, nsink, -1.0, None, ALU.mult))
            v.wait_ge(y_zero, 3)

            def biased(g, s):
                r, w0 = s % 4, (0 if s > 0 else BLK)
                st = scr[:, r, :].rearrange("p (h c) -> p h c", h=4)[:, :, w0:]
                v.wait_ge(s_qk, NB * g + (s + 1))
                if s >= 4:
                    v.wait_ge(s_pt, NB * g + (s - 3))
                nc.vector.tensor_tensor(st, bank(2 * (s % 2), 2).rearrange("p (h c) -> p h c", h=4)[:, :, w0:],
                                        bias[:, :, w0:], ALU.add).then_inc(s_add, 1)

            def maxima(g, s):
                r, w0 = s % 4, (0 if s > 0 else BLK)
                st = scr[:, r, :].rearrange("p (h c) -> p h c", h=4)[:, :, w0:]
                v.wait_ge(s_add, NB * g + (s + 1))
                nc.vector.tensor_reduce(stat[:, r, 0, :], st, AX.X, ALU.max, negate=True).then_inc(mx_link, 1)
                v.wait_ge(mx_link, 2 * NB * g + (2 * s + 1))
                ns = nsink[:, bass.ds(4 * g, 4)]
                nc.vector.tensor_tensor(stat[:, r, 1, :], stat[:, r, 0, :], ns, ALU.min).then_inc(mx_link, 1)
                v.wait_ge(mx_link, 2 * NB * g + (2 * s + 2))
                nc.vector.tensor_tensor(stat[:, r, 4, :], stat[:, r, 1, :], ns, ALU.subtract).then_inc(s_mx, 1)

            def denominators(g, s):
                r = s % 4
                v.wait_ge(s_ex, NB * g + (s + 1))
                nc.vector.tensor_tensor(stat[:, r, 5, :], stat[:, r, 2, :], stat[:, r, 3, :],
                                        ALU.add).then_inc(rd_link, 1)
                v.wait_ge(rd_link, NB * g + (s + 1))
                nc.vector.reciprocal(stat[:, r, 5, :], stat[:, r, 5, :]).then_inc(s_rd, 1)

            def first_blocks(g):
                def bias_there():
                    v.wait_ge(bias_in, 16 * g + 16)
                    biased(g, 0)

                return [bias_there, lambda: maxima(g, 0), lambda: biased(g, 1), lambda: maxima(g, 1),
                        lambda: denominators(g, 0)]

            split(N_SWA + 2, 0, 0)
            for step in first_blocks(0):
                step()

            def attention(g, last):
                n0 = SWA_SLOTS * g + (N_SWA + 2)
                for s in range(2, NB + 5):
                    if s >= 5:
                        b = s - 5
                        v.wait_ge(s_oh, NB * g + (b + 1))
                        o = slice(BLK * b, BLK * (b + 1))
                        nc.vector.tensor_tensor(G_lo[:, 0:2, o],
                                                bank(4 + b % 2)[:, 0:256].rearrange("p (f s) -> p f s", f=2),
                                                G_hi[:, 0:2, o].bitcast(F32), ALU.subtract).then_inc(s_ol, 1)
                    if s < NB:
                        biased(g, s)
                        maxima(g, s)
                    if s <= NB:
                        denominators(g, s - 1)
                    if s == 4:
                        split(n0 + 1, 1, 1)
                if not last:
                    split(n0 + 2, 0, 0)
                    split(n0 + 3, 1, 1)
                    down_step(n0 + 2, 2 * g + D_SWA, 0, [])
                    down_step(n0 + 3, 2 * g + (D_SWA + 1), 1, first_blocks(g + 1) + [lambda: split(n0 + 4, 0, 0)],
                              after=range(TT))

            with v.Fori(0, KVH - 1) as g:
                attention(g, False)
            attention(KVH - 1, True)
            boundary(3, 4, N_FFN1 - 2, D_FFN1 - 2)
            ffn(1, N_FFN1, U_FFN1, D_FFN1, 4)
            boundary(4, None, N_SLOTS - 2, D_FFN1 + 2 * NG - 2)

        @block.gpsimd
        def _(gp):
            def root_mean_squares(b, part):
                if b in (0, 4):
                    order = [(b == 0, t) for t in range(TT)]
                else:
                    order = [(of_x, t - 2 * of_x) for t in range(TT + 2) for of_x in (False, True)
                             if 0 <= t - 2 * of_x < TT]
                chosen = {"all": order, "first half": order[:4], "first": order[:-1], "last": order[-1:]}
                for of_x, t in chosen[part] if isinstance(part, str) else [order[part]]:
                    col, count = t + TT * of_x, squares_done(b, of_x, t)
                    gp.wait_ge(b_sq, count)
                    gp.tensor_scalar(ms[:, col:col + 1], ssq[:, col:col + 1], 1.0 / D, EPS,
                                     ALU.mult, ALU.add).then_inc(b_ms, 1)
                    gp.wait_ge(b_ms, count)
                    gp.tensor_tensor(rs[:, col:col + 1], ms[:, col:col + 1], pows, ALU.pow).then_inc(b_rs, 1)
                    if b > 0 and not of_x and t - 1 in GP_TILES:
                        t -= 1
                        gp.wait_ge(b_y, TT * (b - 1) + t + 1)
                        gp.wait_ge(x_in_sem[t], 16 * (b + 1))
                        gp.tensor_tensor(x_tile(t), x_tile(t), y_acc[:, t, :], ALU.add).then_inc(b_x_gp, 1)

            def turn_lo(number, units, clear=False):
                for i in units:
                    half, k = i // KT, i % KT
                    tok = slice(HALF * half, HALF * (half + 1))
                    gp.wait_ge(h_hi, turn_counts(number) + i + 1)
                    gp.tensor_tensor(H_lo[:, k, tok], modded[:, i % 4, :],
                                     H_hi[:, k, tok].bitcast(F32), ALU.subtract).then_inc(h_lo, 1)
                if clear:
                    gp.memset(y_acc, 0.0).then_inc(y_zero, 1)

            def boundary(b, number, clear=True):
                root_mean_squares(b, "first")
                turn_lo(number, range(AHEAD))
                root_mean_squares(b, "last")
                turn_lo(number, range(AHEAD, 2 * KT), clear)

            gp.memset(pows, -0.5).then_inc(slot_done, 2)
            gp.memset(small[:, 1:2], 0.0).then_inc(u_free, 2)
            gp.memset(small[:, 2:3], 0.0).then_inc(d_free, 2)
            gp.wait_ge(slot_done, 2)
            root_mean_squares(0, "first half")
            for t in range(4, TT):
                root_mean_squares(0, t)
                turn_lo(0, range(2 * t - 8, 2 * t - 6))
            turn_lo(0, range(KT, 2 * KT), clear=True)

            with gp.Fori(0, RH) as h:
                u0 = RET_UPS * h
                for i in range(2):
                    gp.wait_ge(u_free, u0 + (2 * i + 4))
                    a, b = qk[:, 2 * i, :], qk[:, 2 * i + 1, :]
                    gp.tensor_tensor(a, a, scr[:, 2 * i + 1, :], ALU.subtract).then_inc(rot_add, 1)
                    if i == 0:
                        gp.tensor_tensor(b, b, scr[:, 2 * i, :], ALU.add).then_inc(rot_add, 1)
                        gp.wait_ge(rot_add, 4 * h + 2)
                        both = qk[:, 0:2, :].rearrange("p i (c s) -> p (i c) s", c=NC)
                        xi = tab[:, bass.ds(CH * h + T_XI, CH)]
                        gp.tensor_tensor(both, both, xi.unsqueeze(1).to_broadcast([P, 2 * NC, CH]),
                                         ALU.mult).then_inc(rot_add, 1)
                for c in range(NC):
                    gp.wait_ge(a_mv, 8 * h + (c + 1))
                    gp.sem_inc(apart, 1)
                    gp.tensor_scalar(ve[:, c % 2:c % 2 + 1], mv[:, c % 2, 1:2], EPS, None, ALU.add).then_inc(a_ve, 1)
                    gp.wait_ge(a_ve, 8 * h + (c + 1))
                    gp.tensor_tensor(rv[:, c % 2:c % 2 + 1], ve[:, c % 2:c % 2 + 1], pows, ALU.pow).then_inc(a_rs, 1)
                for f in range(4):
                    gp.wait_ge(u_free, u0 + (4 + f + 3))
                    o = head_out[:, f, :, :]
                    gp.tensor_tensor(o, o, state[:, f % 2, :].rearrange("p (c s) -> p c s", c=NC),
                                     ALU.mult).then_inc(g_mul, 1)
                    gp.wait_ge(g_hi, 4 * h + (f + 1))
                    gp.tensor_tensor(G_lo[:, f, :].rearrange("p (c s) -> p c s", c=NC), o,
                                     G_hi[:, f, :].rearrange("p (c s) -> p c s", c=NC).bitcast(F32),
                                     ALU.subtract).then_inc(g_lo, 1)

            boundary(1, 1)
            gp.memset(rel[0:64, :], 1.0).then_inc(r_set, 1)
            gp.dma_start(nsink, sinks_d.to_broadcast([P, QH])).then_inc(ns_in, 16)

            def ffn(layer, u0, g0):
                def tile(f, u, fp, buf):
                    gp.wait_ge(g_sg, f + (FT * layer + 1))
                    gp.wait_ge(u_free, u + 3)
                    m = scr[:, 2 * fp + 1, :]
                    gp.tensor_tensor(m, m, scr[:, 2 * fp, :], ALU.mult).then_inc(g_mul, 1)
                    gp.wait_ge(g_hi, f + (g0 + 1))
                    gp.tensor_tensor(G_lo[:, buf, :], m, G_hi[:, buf, :].bitcast(F32),
                                     ALU.subtract).then_inc(g_lo, 1)

                for f in range(2):
                    tile(f, u0 + 2 * f + 1, f, f)
                with gp.Fori(0, NG // 2) as i:
                    for q in range(4):
                        tile(4 * i + (2 + q), 8 * i + (u0 + 4 + 2 * q + 1), q % 2, (2 + q) % 4)

            ffn(0, U_FFN0, 4 * RH)
            boundary(2, 2, clear=False)
            turn_lo(3, range(2 * KT), clear=True)
            gp.wait_ge(kv_vtok, NB)

            with gp.Fori(0, KVH) as g:
                gp.wait_ge(slot_done, SWA_SLOTS * g + (N_SWA + 2))
                gp.tensor_copy(vg, vtok[:, :, bass.ds(HD * g, HD)]).then_inc(vg_in, 1)
                for s in range(NB):
                    gp.wait_ge(s_rd, NB * g + (s + 1))
                    w0 = 0 if s > 0 else BLK
                    e = scr[:, s % 4, :].rearrange("p (h c) -> p h c", h=4)[:, :, w0:]
                    gp.tensor_tensor(e, e, stat[:, s % 4, 5, :].unsqueeze(2).to_broadcast([P, 4, 256 - w0]),
                                     ALU.mult).then_inc(s_p, 1)

            boundary(3, 4)
            ffn(1, U_FFN1, 4 * RH + FT)
            root_mean_squares(4, "all")


def _tables():
    f4 = np.float32
    inv = f4(10000.0) ** (-np.arange(P, dtype=f4) / f4(P))
    ang = (np.arange(S, dtype=f4)[None, :] * inv[:, None]).astype(f4)
    rope = np.stack([np.cos(ang), np.sin(ang)], 1).astype(f4).reshape(P, 2 * S)
    gamma = 1.0 - 2.0 ** (-5.0 - np.arange(RH))
    i = np.arange(CH)
    tab = np.zeros((P, N_TAB))
    tab[:, T_XI:T_XI + RH * CH] = (gamma[:, None] ** (i + 1)).reshape(1, -1)
    tab[:, T_GINV:T_GINV + RH] = gamma[None, :] ** -(i[:, None] + 1.0) * DK ** -0.5
    tab[:, T_ZETA:T_ZETA + RH] = gamma[None, :] ** (CH - 1.0 - i[:, None]) * DK ** -0.5
    tab[:, T_GC:T_GC + RH] = gamma[None, :] ** float(CH)
    tab[:, T_TRI:T_TRI + CH] = i[None, :] >= i[:, None]
    tab[:, T_ID:T_ID + P] = np.eye(P)
    tab[:, T_ONES:T_ONES + P] = 1.0
    n = np.arange(BLK)
    large = 16 + (np.log(np.maximum(n, 1).astype(f4) / 16) / math.log(128 / 16) * 16).astype(np.int32)
    bucket = np.where(n < 16, n, np.minimum(large, 31))
    hot = np.zeros((33, ML))
    for w in range(ML):
        dist = 255 - w
        if 0 <= dist < BLK:
            hot[bucket[dist], w] = 1.0
        else:
            hot[32, w] = NEG
    return rope, tab.astype(f4), hot.astype(f4)


def _up(w, f):
    return w[:, f].reshape(KT, P, P).transpose(1, 0, 2).reshape(P, 1024)


def _down(w, f, half):
    return w[P * f:P * (f + 2), HALF * half:HALF * (half + 1)].reshape(2, P, HALF).transpose(1, 0, 2).reshape(P, 1024)


def _ada(w, v, k):
    return w[:, D * v + P * k:D * v + P * (k + 1)].T


def _stream(a):
    vectors = [(a["ada_w"][0], v) for v in range(6)] + [(a["kv_ada_w"], v) for v in range(2)] \
        + [(a["ada_w"][1], v) for v in range(6)]
    win, wout = a["ret_w_in"][0], a["ret_w_out"][0]
    slots = []
    for h in range(RH + 1):
        if h > 0:
            slots += [_down(wout, 4 * (h - 1) + 2 * g, half) for g in range(2) for half in range(2)]
        if h < RH:
            starts = [DK * h + P * i for i in range(2)] + [D + DK * h + P * i for i in range(2)] \
                + [4 * D + DV * h + P * i for i in range(4)]
            ups = [_up(win, slice(s, s + P)) for s in starts]
            wv = win[:, 2 * D + DV * h:2 * D + DV * (h + 1)]
            slots += ups[:4] + [_down(wv, k, 0) for k in range(0, KT, 2)] + ups[4:]

    def ffn(layer):
        up, down, made = a["ffn_w_up"][layer], a["ffn_w_down"][layer], []

        def ups(g):
            return [_up(up, slice(P * (f + FT * val), P * (f + FT * val + 1))) for f in (2 * g, 2 * g + 1)
                    for val in range(2)]

        def downs(g):
            return [_down(down, 2 * g, half) for half in range(2)]

        made += ups(0)
        for g in range(1, NG):
            made += ups(g) + downs(g - 1)
        return made + downs(NG - 1)

    slots += ffn(0)
    slots += [_up(a["kv_w"], slice(P * f, P * (f + 1))) for f in range(4)]
    wq, wo = a["swa_w_q"][0], a["swa_w_o"][0]
    groups = [[np.r_[HD * (4 * g + i):HD * (4 * g + i + 1), HD * (4 * g + 2 + i):HD * (4 * g + 3 + i)]
               for i in range(2)] for g in range(KVH)]
    slots += [_up(wq, features) for features in groups[0]]
    for g in range(KVH):
        if g < KVH - 1:
            slots += [_up(wq, features) for features in groups[g + 1]]
        slots += [_down(wo[np.concatenate(groups[g])], 0, half) for half in range(2)]
    slots += ffn(1)
    assert len(slots) == N_SLOTS

    units = [_ada(w, v, k) for w, v in vectors for k in range(KT)]
    first, units = units[:N_FIRST], units[N_FIRST:]
    pieces, slots = slots[:RET_FIRST], slots[RET_FIRST:]
    for h in range(RH):
        for j in range(RET_SLOTS if h < RH - 1 else RET_SLOTS - 2):
            pieces.append(slots.pop(0))
            pieces += units[:ADA_UNITS.get(j, 0)]
            units = units[ADA_UNITS.get(j, 0):]
    pieces += slots
    assert len(pieces) == N_ENTRIES and not units
    return np.stack(first), np.stack(pieces)


def _columns(a):
    vectors = [a["ada_b"][0], a["kv_ada_b"], a["ada_b"][1], a["norm_g"].reshape(-1), a["kv_norm_g"],
               a["ffn_conv_w"].reshape(-1), a["ffn_conv_b"].reshape(-1)]
    return np.ascontiguousarray(np.concatenate(vectors).reshape(N_COLS, P).T)


def kernel(**inputs):
    import concourse.bacc as bacc
    from concourse.bass_utils import run_bass_kernel_spmd

    a = {name: np.asarray(value) for name, value in inputs.items()}
    rope, tab, hot = _tables()
    first, stream = _stream(a)
    arrays = {
        "x": np.ascontiguousarray(a["x"][0]), "c": a["c"], "cols": _columns(a), "first": first, "stream": stream,
        "sinks": a["swa_sinks"], "rel": a["rel_bias"], "rope": rope, "tab": tab, "hot": hot,
    }
    nc = bacc.Bacc("TRN2", target_bir_lowering=False, num_devices=1)
    args = [nc.dram_tensor(f"in_{name}", value.shape, mybir.dt.from_np(value.dtype), kind="ExternalInput").ap()
            for name, value in arrays.items()]
    out = nc.dram_tensor("out", (S, D), F32, kind="ExternalOutput").ap()
    trunk(nc, *args, out)
    run = run_bass_kernel_spmd(nc, [{f"in_{name}": value for name, value in arrays.items()}], core_ids=[0])
    return run.results[0]["out"].reshape(1, S, D)
```
